# Optimizing a Trainium2 kernel written in Bass

```python
import jax, jax.numpy as jnp
from jax import lax
import numpy as np

D_MODEL = 1024
BATCH = 1
SEQ = 512
DEPTH = 2

N_MIXERS = 2
N_MLA_LAYERS = (DEPTH + N_MIXERS - 1) // N_MIXERS
N_RNN_LAYERS = DEPTH // N_MIXERS

N_HEADS = 16
Q_LORA = 384
KV_LORA = 256
QK_NOPE = 64
QK_ROPE = 32
QK_HEAD = QK_NOPE + QK_ROPE
V_HEAD = 64
ROPE_THETA = 10000.0
Q_BLOCK = 128

D_RNN = D_MODEL
RNN_BLOCKS = 4
RNN_BW = D_RNN // RNN_BLOCKS
CONV_W = 4
LRU_C = 8.0

N_EXPERTS = 32
N_GROUPS = 8
EXPERTS_PER_GROUP = N_EXPERTS // N_GROUPS
TOP_K = 2
D_EXPERT = 512
MOE_BLOCK = 128

EPS = 1e-6

kernel_name = "hybrid_mla_rglru_grouped_moe_adaln"

def rmsnorm(x, g):
    xf = x.astype(jnp.float32)
    y = xf * lax.rsqrt(jnp.mean(xf * xf, axis=-1, keepdims=True) + EPS)
    return (y * g.astype(jnp.float32)).astype(x.dtype)

def modulate(x, g, shift, scale):
    return rmsnorm(x, g) * (1 + scale[:, None, :]) + shift[:, None, :]

def rope(x, cos, sin):
    x1, x2 = jnp.split(x, 2, axis=-1)
    c = cos.astype(x.dtype)
    s = sin.astype(x.dtype)
    return jnp.concatenate([x1 * c - x2 * s, x1 * s + x2 * c], axis=-1)

def mla_mixer(h, cos, sin, w_in, q_a_norm, kv_a_norm, w_q_b, w_kv_b, q_norm, k_norm, w_o):
    B, S, _ = h.shape
    lat = h @ w_in
    q_lat, kv_lat, k_pe = jnp.split(lat, [Q_LORA, Q_LORA + KV_LORA], axis=-1)
    q = (rmsnorm(q_lat, q_a_norm) @ w_q_b).reshape(B, S, N_HEADS, QK_HEAD)
    kv = (rmsnorm(kv_lat, kv_a_norm) @ w_kv_b).reshape(B, S, N_HEADS, QK_NOPE + V_HEAD)
    k_nope, v = jnp.split(kv, [QK_NOPE], axis=-1)
    k = jnp.concatenate([k_nope, jnp.broadcast_to(k_pe[:, :, None, :], (B, S, N_HEADS, QK_ROPE))], axis=-1)
    q = rmsnorm(q, q_norm)
    k = rmsnorm(k, k_norm)
    c4 = cos[:, :, None, :]
    s4 = sin[:, :, None, :]
    q = jnp.concatenate([q[..., :QK_NOPE], rope(q[..., QK_NOPE:], c4, s4)], axis=-1)
    k = jnp.concatenate([k[..., :QK_NOPE], rope(k[..., QK_NOPE:], c4, s4)], axis=-1)
    scale = QK_HEAD ** -0.5
    nqb = S // Q_BLOCK
    qb = q.reshape(B, nqb, Q_BLOCK, N_HEADS, QK_HEAD).transpose(1, 0, 2, 3, 4)

    def attend(q_blk):
        s = jnp.einsum('bqhd,bkhd->bhqk', q_blk, k, preferred_element_type=jnp.float32) * scale
        p = jax.nn.softmax(s, axis=-1).astype(v.dtype)
        return jnp.einsum('bhqk,bkhd->bqhd', p, v)

    o = lax.map(attend, qb)
    o = o.transpose(1, 0, 2, 3, 4).reshape(B, S, N_HEADS * V_HEAD)
    return o @ w_o

def dwconv_centred(x, w, b):
    S = x.shape[1]
    left = CONV_W // 2
    xp = jnp.pad(x, ((0, 0), (left, CONV_W - 1 - left), (0, 0)))
    return sum(xp[:, k:k + S] * w[k] for k in range(CONV_W)) + b

def block_diag(x, w, b):
    B, S, _ = x.shape
    xb = x.reshape(B, S, RNN_BLOCKS, RNN_BW)
    return jnp.einsum('bsnd,nde->bsne', xb, w).reshape(B, S, D_RNN) + b

def _lru_combine(e1, e2):
    a1, b1 = e1
    a2, b2 = e2
    return a1 * a2, a2 * b1 + b2

def lru_scan(xc, lam, w_r, b_r, w_i, b_i, reverse):
    f32 = jnp.float32
    r = jax.nn.sigmoid(block_diag(xc, w_r, b_r).astype(f32))
    i = jax.nn.sigmoid(block_diag(xc, w_i, b_i).astype(f32))
    log_a = -LRU_C * r * jax.nn.softplus(-lam.astype(f32))
    a = jnp.exp(log_a)
    mult = jnp.sqrt(-jnp.expm1(2.0 * log_a))
    S = xc.shape[1]
    first = (jnp.arange(S) == (S - 1 if reverse else 0))[None, :, None]
    mult = jnp.where(first, 1.0, mult)
    bx = mult * i * xc.astype(f32)
    _, hs = lax.associative_scan(_lru_combine, (a, bx), reverse=reverse, axis=1)
    return hs

def rglru_mixer(h, w_in, conv_w, conv_b, lam_f, w_rf, b_rf, w_if, b_if, lam_b, w_rb, b_rb, w_ib, b_ib, w_o):
    gate, xb = jnp.split(h @ w_in, 2, axis=-1)
    xc = dwconv_centred(xb, conv_w, conv_b)
    hf = lru_scan(xc, lam_f, w_rf, b_rf, w_if, b_if, reverse=False)
    hb = lru_scan(xc, lam_b, w_rb, b_rb, w_ib, b_ib, reverse=True)
    y = jax.nn.gelu(gate) * (hf + hb).astype(h.dtype)
    return y @ w_o

def route(xt, w_router, router_bias):
    T = xt.shape[0]
    scores = jax.nn.sigmoid(jnp.dot(xt, w_router, preferred_element_type=jnp.float32))
    biased = scores + router_bias.astype(jnp.float32)
    grp = biased.reshape(T, N_GROUPS, EXPERTS_PER_GROUP)
    gscore = lax.top_k(grp, TOP_K)[0].sum(-1)
    g_sel = jnp.argmax(gscore, axis=-1)
    in_group = (jnp.arange(N_EXPERTS) // EXPERTS_PER_GROUP)[None, :] == g_sel[:, None]
    masked = jnp.where(in_group, biased, -jnp.inf)
    _, idx = lax.top_k(masked, TOP_K)
    w = jnp.take_along_axis(scores, idx, axis=-1)
    w = w / jnp.sum(w, axis=-1, keepdims=True)
    return idx, w

def moe(xt, idx, wts, w_gu, w_dn):
    T, D = xt.shape
    A = T * TOP_K
    P = A + N_EXPERTS * MOE_BLOCK
    nb = P // MOE_BLOCK
    e_flat = idx.reshape(A)
    order = jnp.argsort(e_flat)
    e_sorted = e_flat[order]
    counts = jnp.bincount(e_flat, length=N_EXPERTS)
    start = jnp.cumsum(counts) - counts
    padded = ((counts + MOE_BLOCK - 1) // MOE_BLOCK) * MOE_BLOCK
    pend = jnp.cumsum(padded)
    pstart = pend - padded
    dest_sorted = pstart[e_sorted] + (jnp.arange(A) - start[e_sorted])
    dest = jnp.zeros((A,), jnp.int32).at[order].set(dest_sorted.astype(jnp.int32))
    row_tok = jnp.full((P,), T, jnp.int32).at[dest].set((jnp.arange(A) // TOP_K).astype(jnp.int32))
    xs = jnp.concatenate([xt, jnp.zeros((1, D), xt.dtype)], axis=0)[row_tok]
    blk_exp = jnp.minimum(jnp.searchsorted(pend, jnp.arange(nb) * MOE_BLOCK, side='right'), N_EXPERTS - 1)

    def expert_block(args):
        xb, e = args
        g, u = jnp.split(xb @ w_gu[e], 2, axis=-1)
        return (jax.nn.silu(g) * u) @ w_dn[e]

    ys = lax.map(expert_block, (xs.reshape(nb, MOE_BLOCK, D), blk_exp)).reshape(P, D)
    y = ys[dest].reshape(T, TOP_K, D)
    return jnp.einsum('tk,tkd->td', wts.astype(y.dtype), y)

def _normal(k, shape, fan_in, scale=1.0):
    return jax.random.normal(k, shape, jnp.float32) * (scale * fan_in ** -0.5)

def _gain(k, shape):
    return 1.0 + 0.05 * jax.random.normal(k, shape, jnp.float32)

def _small(k, shape, s=0.02):
    return s * jax.random.normal(k, shape, jnp.float32)

def _lru_lambda(k, shape):
    a0 = jax.random.uniform(k, shape, jnp.float32, 0.9, 0.999)
    p = a0 ** (1.0 / LRU_C)
    return jnp.log(p) - jnp.log1p(-p)

def setup_inputs(seed: int = 0) -> dict:
    key = jax.random.key(seed)
    ks = iter(jax.random.split(key, 48))
    NM, NR = N_MLA_LAYERS, N_RNN_LAYERS
    d = {}
    d['x'] = jax.random.normal(next(ks), (BATCH, SEQ, D_MODEL), jnp.float32)
    d['c'] = jax.random.normal(next(ks), (BATCH, D_MODEL), jnp.float32)
    offs = jax.random.randint(next(ks), (BATCH, 1), 0, 1024, jnp.int32)
    d['positions'] = (offs + jnp.arange(SEQ, dtype=jnp.int32)[None, :]).astype(jnp.int32)
    d['norm_mix'] = _gain(next(ks), (DEPTH, D_MODEL))
    d['norm_ffn'] = _gain(next(ks), (DEPTH, D_MODEL))
    d['w_ada'] = _normal(next(ks), (DEPTH, D_MODEL, 6 * D_MODEL), D_MODEL, 0.5)
    d['b_ada'] = _small(next(ks), (DEPTH, 6 * D_MODEL))
    d['mla_w_in'] = _normal(next(ks), (NM, D_MODEL, Q_LORA + KV_LORA + QK_ROPE), D_MODEL)
    d['mla_q_a_norm'] = _gain(next(ks), (NM, Q_LORA))
    d['mla_kv_a_norm'] = _gain(next(ks), (NM, KV_LORA))
    d['mla_w_q_b'] = _normal(next(ks), (NM, Q_LORA, N_HEADS * QK_HEAD), Q_LORA)
    d['mla_w_kv_b'] = _normal(next(ks), (NM, KV_LORA, N_HEADS * (QK_NOPE + V_HEAD)), KV_LORA)
    d['mla_q_norm'] = _gain(next(ks), (NM, QK_HEAD))
    d['mla_k_norm'] = _gain(next(ks), (NM, QK_HEAD))
    d['mla_w_o'] = _normal(next(ks), (NM, N_HEADS * V_HEAD, D_MODEL), N_HEADS * V_HEAD)
    d['rnn_w_in'] = _normal(next(ks), (NR, D_MODEL, 2 * D_RNN), D_MODEL)
    d['rnn_conv_w'] = _normal(next(ks), (NR, CONV_W, D_RNN), CONV_W)
    d['rnn_conv_b'] = _small(next(ks), (NR, D_RNN))
    d['rnn_lam_f'] = _lru_lambda(next(ks), (NR, D_RNN))
    d['rnn_w_rf'] = _normal(next(ks), (NR, RNN_BLOCKS, RNN_BW, RNN_BW), RNN_BW)
    d['rnn_b_rf'] = _small(next(ks), (NR, D_RNN), 0.1)
    d['rnn_w_if'] = _normal(next(ks), (NR, RNN_BLOCKS, RNN_BW, RNN_BW), RNN_BW)
    d['rnn_b_if'] = _small(next(ks), (NR, D_RNN), 0.1)
    d['rnn_lam_b'] = _lru_lambda(next(ks), (NR, D_RNN))
    d['rnn_w_rb'] = _normal(next(ks), (NR, RNN_BLOCKS, RNN_BW, RNN_BW), RNN_BW)
    d['rnn_b_rb'] = _small(next(ks), (NR, D_RNN), 0.1)
    d['rnn_w_ib'] = _normal(next(ks), (NR, RNN_BLOCKS, RNN_BW, RNN_BW), RNN_BW)
    d['rnn_b_ib'] = _small(next(ks), (NR, D_RNN), 0.1)
    d['rnn_w_o'] = _normal(next(ks), (NR, D_RNN, D_MODEL), D_RNN)
    d['w_router'] = _normal(next(ks), (D_MODEL, N_EXPERTS), D_MODEL)
    d['router_bias'] = _small(next(ks), (N_EXPERTS,), 0.01)
    d['moe_w_gu'] = _normal(next(ks), (DEPTH, N_EXPERTS, D_MODEL, 2 * D_EXPERT), D_MODEL)
    d['moe_w_dn'] = _normal(next(ks), (DEPTH, N_EXPERTS, D_EXPERT, D_MODEL), D_EXPERT)
    return d

def reference(x, c, positions, norm_mix, norm_ffn, w_ada, b_ada,
              mla_w_in, mla_q_a_norm, mla_kv_a_norm, mla_w_q_b, mla_w_kv_b, mla_q_norm, mla_k_norm, mla_w_o,
              rnn_w_in, rnn_conv_w, rnn_conv_b,
              rnn_lam_f, rnn_w_rf, rnn_b_rf, rnn_w_if, rnn_b_if,
              rnn_lam_b, rnn_w_rb, rnn_b_rb, rnn_w_ib, rnn_b_ib, rnn_w_o,
              w_router, router_bias, moe_w_gu, moe_w_dn):
    B, S, D = x.shape
    half = QK_ROPE // 2
    inv_freq = ROPE_THETA ** (-jnp.arange(half, dtype=jnp.float32) / half)
    ang = positions.astype(jnp.float32)[..., None] * inv_freq
    cos, sin = jnp.cos(ang), jnp.sin(ang)
    c_act = jax.nn.silu(c)
    for i in range(DEPTH):
        mod = c_act @ w_ada[i] + b_ada[i]
        sh1, sc1, g1, sh2, sc2, g2 = jnp.split(mod, 6, axis=-1)
        h = modulate(x, norm_mix[i], sh1, sc1)
        j = i // N_MIXERS
        if i % N_MIXERS == 0:
            m = mla_mixer(h, cos, sin, mla_w_in[j], mla_q_a_norm[j], mla_kv_a_norm[j], mla_w_q_b[j],
                          mla_w_kv_b[j], mla_q_norm[j], mla_k_norm[j], mla_w_o[j])
        else:
            m = rglru_mixer(h, rnn_w_in[j], rnn_conv_w[j], rnn_conv_b[j],
                            rnn_lam_f[j], rnn_w_rf[j], rnn_b_rf[j], rnn_w_if[j], rnn_b_if[j],
                            rnn_lam_b[j], rnn_w_rb[j], rnn_b_rb[j], rnn_w_ib[j], rnn_b_ib[j], rnn_w_o[j])
        x = x + g1[:, None, :] * m
        h = modulate(x, norm_ffn[i], sh2, sc2)
        ht = h.reshape(B * S, D)
        idx, wts = route(ht, w_router, router_bias)
        y = moe(ht, idx, wts, moe_w_gu[i], moe_w_dn[i])
        x = x + g2[:, None, :] * y.reshape(B, S, D)
    return x


_drawn_inputs = setup_inputs


def setup_inputs(seed=0):
    import zlib

    import numpy as np

    out = dict(_drawn_inputs(seed))
    spreads = {}
    factors = {'mla_q_a_norm': 6.189,
     'mla_q_norm': 7.102,
     'mla_k_norm': 8.0,
     'rnn_b_rf': 4.809,
     'rnn_b_if': 3.072,
     'rnn_b_rb': 6.527}
    for name, (base, spread) in spreads.items():
        noise = np.random.default_rng([zlib.crc32(name.encode()), seed]).standard_normal(out[name].shape)
        drawn = base * np.exp(spread * noise) if base else spread * noise
        out[name] = __import__('jax').numpy.asarray(drawn.astype(out[name].dtype))
    for name, factor in factors.items():
        out[name] = (out[name] * factor).astype(out[name].dtype)
    return out
```

```python
from contextlib import ExitStack

import numpy as np
import concourse.bass as bass
from concourse import mybir

P = 128
F32 = mybir.dt.float32
I32 = mybir.dt.int32
ALU = mybir.AluOpType
ACT = mybir.ActivationFunctionType
AX = mybir.AxisListType

D = 1024
SEQ = 512
KT = D // P
TT = SEQ // P
HALF = 512
H = 16
QL, KVL, ROPE, NOPE, VH = 384, 256, 32, 64, 64
QK = NOPE + ROPE
LAT = QL + KVL + ROPE
RH = ROPE // 2
NE, NG, EPG = 32, 8, 4
FE = 512
FT = FE // P
NBLK = 4
EPS = 1e-6
FAR = 1e30
GELU_SCALE = 2.0 * float(np.sqrt(2.0 / np.pi))
TWO_PI = float(2.0 * np.pi)
ROUNDER = 1.5 * 2.0 ** 23
PI_IN = 3.1415925
_p0 = float(np.floor(TWO_PI * 2 ** 7) / 2 ** 7)
_p1 = float(np.floor((TWO_PI - _p0) * 2 ** 18) / 2 ** 18)
PI_PARTS = (_p0, _p1, TWO_PI - _p0 - _p1)
LRU_C = 8.0
MAX_EXTRA = 7
SKIP = 1 << 20

VROW = {}
VCOUNT = {}
_n = 0
for _name, _rows in (("norm_mix", 16), ("norm_ffn", 16), ("conv_w", 32), ("conv_b", 8), ("lam_f", 8), ("b_rf", 8),
                     ("b_if", 8), ("lam_b", 8), ("b_rb", 8), ("b_ib", 8)):
    VROW[_name] = _n
    VCOUNT[_name] = _rows
    _n += _rows
NVROW = _n

STAGES = {}
OWNER = []


def _stage(name, owners):
    STAGES[name] = len(OWNER)
    OWNER.extend(owners)


_stage("setup", "DDD")
_stage("cols0", "DD")
_stage("norm0", "AD" * 4)
_stage("lat", "AD" * 4)
_stage("latT", "ADADA")
_stage("q", "A" * 12)
_stage("ffncols0", "DD")
_stage("kv", "A" * 16)
_stage("gate0", "DDDD")
_stage("oT", "AD" * 4)
_stage("proj0", "D" * 8)
_stage("norm1", "AD" * 4)
_stage("logits0", "A")
_stage("rank0", "DD")
_stage("ada1", "D" + "A" * 4)
_stage("norm2", "AD" * 4)
_stage("xb0", "DD")
for _b in range(NBLK):
    _stage(f"gate_r{_b}", "AA")
    if _b < NBLK - 1:
        _stage(f"xb{_b + 1}", "DD")
    _stage(f"rg{_b}", "A" * 8)
_stage("proj1", "D" * 8)
_stage("norm3", "AD" * 4)
_stage("logits1", "A")
_stage("rank1", "DD")


def evacuated(g):
    who = OWNER[g]
    return who, sum(1 for o in OWNER[:g + 1] if o == who)


def trunk(nc, x, c, positions, norm_mix, norm_ffn, w_ada, b_ada, mla_w_in, mla_q_a_norm, mla_kv_a_norm,
          mla_w_q_b, mla_w_kv_b, mla_q_norm, mla_k_norm, mla_w_o, rnn_w_in, rnn_conv_w, rnn_conv_b,
          rnn_lam_f, rnn_w_rf, rnn_b_rf, rnn_w_if, rnn_b_if, rnn_lam_b, rnn_w_rb, rnn_b_rb, rnn_w_ib,
          rnn_b_ib, rnn_w_o, w_router, router_bias, moe_w_gu, moe_w_dn, out):
    ctx = ExitStack()
    with ctx:
        def sb(name, shape, dt=F32):
            return ctx.enter_context(nc.sbuf_tensor(name, shape, dt))

        def sem(name):
            return ctx.enter_context(nc.semaphore(name))

        ps = ctx.enter_context(nc.psum_tensor("ps", [P, 8, HALF], F32))
        ring_gu0 = sb("ring_gu0", [P, KT * D])
        ring_dn0 = sb("ring_dn0", [P, FT * D])
        ring_dn1 = sb("ring_dn1", [P, FT * D])
        ring_gu1 = sb("ring_gu1", [P, KT * D])
        ring_gu = (ring_gu0, ring_gu1)
        ring_dn = (ring_dn0, ring_dn1)
        arena = sb("arena", [P, 18944])
        x_tok = sb("x_tok", [P, TT, D])
        gate_bc = sb("gate_bc", [P, 2, D])
        ident = sb("ident", [P, P])
        ones = sb("ones", [P, P])
        before = sb("before", [P, P])
        pick = sb("pick", [2, 2, P])
        gate_bias = ring_dn0[0:2, 3072:3072 + D]
        vrows = arena[0:NVROW, 0:P]
        vcols = sb("vcols", [P, NVROW])
        brows = arena[0:48, P:2 * P]
        bcols = sb("bcols", [P, 48])
        mrows = arena[0:7, 2 * P:3 * P]
        mcols = sb("mcols", [P, 7])
        c_raw = sb("c_raw", [P, KT])
        c_act = sb("c_act", [P, KT])
        scale_col = sb("scale_col", [P, 4, KT])
        shift_col = sb("shift_col", [P, 4, KT])
        ss = sb("ss", [P, TT])
        std = sb("std", [P, TT])
        rstd = sb("rstd", [P, TT])
        eps = sb("eps", [P, 1])
        ropeg = sb("ropeg", [P, 2, ROPE])
        pos_i = sb("pos_i", [P, TT], I32)
        router_w = sb("router_w", [P, KT, NE])
        rbias = sb("rbias", [P, NE])
        down_e = sb("down_e", [P, TT, NE])
        up_e = sb("up_e", [P, TT, NE])
        down_g = sb("down_g", [P, TT, NG])
        tokval = sb("tokval", [P, TT, 2], I32)
        more_id = sb("more_id", [P, 3 * NE])
        rs_small = sb("rs_small", [P, 12, TT])
        chosen = sb("chosen", [P, TT, NE])
        wts = sb("wts", [P, TT, 2])
        dest = sb("dest", [P, TT, 2], I32)
        slot_val = sb("slot_val", [P, 4, NE], I32)
        slot_tok = sb("slot_tok", [P, 4, NE], I32)
        empty = arena[:, 18432:18432 + P].bitcast(I32)
        idx_in = sb("idx_in", [P, 3], I32)
        idx_out = sb("idx_out", [P, 3], I32)
        more_f = sb("more_f", [1, 32])
        more_i = sb("more_i", [1, 32], I32)
        tick = sb("tick", [P, 1])
        lam_t = sb("lam_t", [P, 4, 2 * KT])

        xn_dram = nc.dram_tensor("xn_dram", [SEQ, D], F32)
        table_dram = [nc.dram_tensor(f"table{l}_dram", [SEQ * NE, 1], I32).ap() for l in range(2)]
        ys_dram = nc.dram_tensor("ys_dram", [2 * SEQ, D], F32)
        xn_dram, ys_dram = xn_dram.ap(), ys_dram.ap()

        def view(t, off, *dims):
            n = 1
            for d in dims:
                n *= d
            v = t[:, off:off + n]
            if len(dims) == 2:
                v = v.rearrange("p (a b) -> p a b", a=dims[0])
            elif len(dims) == 3:
                v = v.rearrange("p (a b c) -> p a b c", a=dims[0], b=dims[1])
            assert len(dims) < 4
            return v

        hT = view(arena, 0, KT, SEQ)
        w_in = view(arena, 4096, KT, LAT)
        w_qb = view(arena, 9728, 3, H * QK)
        q_tok = view(arena, 0, TT, H, QK)
        kv_tok = view(arena, 6144, TT, H, NOPE + VH)
        latT = view(arena, 14336, 5, SEQ)
        xn_mla = view(arena, 14336, TT, D)
        lat = view(ring_dn1, 0, TT, LAT)
        w_kvb = view(ring_dn1, 0, 2, H * (NOPE + VH))
        o_tok = view(ring_dn1, 0, TT, D)
        w_o = view(ring_gu1, 0, KT, D)
        oT = view(arena, 0, KT, SEQ)
        probs = view(arena, 16896, 2, SEQ)
        probsT = view(arena, 17920, 2, TT, P)
        qn = view(ring_dn0, 0, 2, TT, QK)
        kn = view(ring_dn0, 768, 2, TT, QK)
        qT = view(ring_dn0, 1536, 2, SEQ)
        kT = view(ring_dn0, 2560, 2, SEQ)
        rope_tmp = view(ring_gu1, 0, 4, TT * H * RH)
        sq_tmp = view(ring_dn0, 0, 2, H * QK)
        lat_sq_tmp = view(arena, 16896, QL)
        mla_small = sb("mla_small", [P, 576])
        trig = arena[:, 17408:17408 + 5 * TT * RH].rearrange("p (n i j) -> p n i j", n=5, i=TT)
        inv_freq = view(mla_small, 0, RH)
        pos_f = view(mla_small, 16, TT)
        table = view(mla_small, 20, 8, TT * RH)
        rope_c1q, rope_s2q, rope_s1q, rope_c2q, rope_c1k, rope_s2k, rope_s1k, rope_c2k = [
            table[:, n, :].rearrange("p (a b) -> p a b", a=TT) for n in range(8)]
        nmax = view(mla_small, 532, 4)
        rsum = view(mla_small, 536, 2, TT)
        rrec = view(mla_small, 544, TT)
        lat_ss = view(mla_small, 548, 2, TT)
        lat_r = view(mla_small, 556, 2, TT)
        pe_ss = view(mla_small, 564, TT)
        mla_big = sb("mla_big", [P, 2 * TT * H + 2 * TT * ROPE])
        rq = view(mla_big, 0, TT, H)
        rk = view(mla_big, TT * H, TT, H)
        k_pe = view(mla_big, 2 * TT * H, TT, ROPE)
        k_pe_raw = view(mla_big, 2 * TT * H + TT * ROPE, TT, ROPE)
        q_gain = view(mla_small, 568, 1)
        q_flat = view(arena, 0, TT * H * QK)
        kv_flat = view(arena, 6144, TT * H * (NOPE + VH))
        o_heads = view(ring_dn1, 0, TT, H, VH)
        rope_k_tmp = view(arena, 17728, 4, TT * RH)
        prod = view(arena, 16896, 2, HALF)
        w_xb = view(arena, 4096, KT, 2 * P)
        w_gt = view(arena, 6144, KT, 2 * P)
        w_rg = view(arena, 8192, 8, 2 * P)
        xn_rnn = view(arena, 10240, TT, D)
        pad = SEQ + 3
        xb_pad = view(arena, 10240, 2, pad)
        xc_ = [view(ring_gu0, n * 2 * SEQ, 2, SEQ) for n in range(2)]
        gate_ = [view(ring_gu0, (2 + n) * 2 * SEQ, 2, SEQ) for n in range(2)]
        gtmp = view(arena, 13320, 2, SEQ)
        r_s = view(arena, 14344, 4, SEQ)
        i_s = view(arena, 16392, 4, SEQ)
        t_s = view(ring_dn0, 0, 4, SEQ)
        rc_s = view(ring_dn0, 2048, 4, SEQ)
        yT = view(ring_dn1, 0, KT, SEQ)
        scores = view(arena, 16384, TT, NE)
        biased = view(arena, 16512, TT, NE)
        pairs = view(arena, 16640, TT * NG, 6)
        gs = arena[:, 16832:16832 + 3 * TT * NG].rearrange("p (n i g) -> p n i g", n=3, i=TT)
        rt = arena[:, 16928:16928 + 7 * TT * NE].rearrange("p (n i e) -> p n i e", n=7, i=TT)
        more = arena[0:1, 17824:17824 + 6 * 3 * NE].rearrange("p (n e) -> p n e", n=6)
        stage = view(arena, 0, 2, 3072)
        acc1 = view(arena, 6144, 2, 3072)
        acc1_flat = view(arena, 6144, 6 * D)
        xn_moe = view(arena, 12288, TT, D)
        xg = view(arena, 12288, 2, D)
        xgT = view(arena, 14336, KT, P)
        yo = view(arena, 15360, 2, D)
        hmid = view(arena, 17408, FE)
        hmidT = view(arena, 17920, FT, P)
        hsil = view(arena, 18432, FE)
        y_pair = view(arena, 12288, 2, 2 * D)
        y_tmp = view(arena, 16384, 2, D)
        lam_c = sb("lam_c", [P, 2, KT])

        first_s = sb("first_s", [P, 4])

        S = {}
        for name in (
                "x_in", "c_in", "rows_in", "misc_in", "brow_in", "pool_const", "mrow_set", "mrow_in", "c_ready", "ada_in0", "ada_in1",
                "ada_used", "unit", "a_free", "d_free", "dve_order", "act_order", "pool_order", "pool_step", "cols_set",
                "mod_ready", "resid_ready", "ss_ready", "rstd_ready", "xn_ready", "w_in_in", "w_qb_in", "w_kvb_in",
                "w_o_in", "angle_ready", "trig_ready", "ropeq_done", "lat_stat", "lat_scaled", "sq_ready", "sq_used", "qk_var",
                "qk_std", "rope_done", "qkn_ready", "qkT_made", "qT_ready", "kT_ready", "s_ready", "nmax_ready",
                "p_ready", "pT_made", "pT_a", "pT_d", "pv_done", "rrec_ready", "o_done", "router_in",
                "scores_ready", "chosen_ready", "dest_ready", "table_empty", "table_put", "xn_saved", "table_in",
                "slots_ready", "xg_clear", "idx_in_set", "idx_out_set", "gathered0", "gathered1", "scattered0",
                "scattered1", "gu_in0", "gu_in1", "dn_in0", "dn_in1", "gu_done", "dn_done", "xT_made", "hT_made",
                "xT_a", "xT_d", "sil_ready", "hmid_ready", "hmidT_ready", "yo_a", "yo_d", "stage_in0", "stage_in1",
                "stage_used", "acc1_zero", "acc1_bias", "y_in0", "y_in1", "y_used", "y_first", "ov_done", "out_done",
                "wx_in", "wg_in", "wr_in", "xc_ready", "gz_ready", "gs_ready", "gelu_ready", "t_ready", "rc_ready", "st_ready",
                "y_ready", "lam_abs", "lam_exp"):
            S[name] = ctx.enter_context(nc.semaphore(name))
        OV = [{n: ctx.enter_context(nc.semaphore(f"more{l}_{n}")) for n in (
            "w_in", "idx", "gathered", "xT_made", "xT_ready", "gu_done", "sil", "hmid", "hT_made", "hmidT",
            "dn_done", "yo_a", "yo_d", "scattered")} for l in range(2)]

        block = ctx.enter_context(nc.Block())

        def bank(g):
            return ps[:, g % 8, :]

        def counts(value):
            return not (isinstance(value, int) and value <= 0)

        def emptied(g):
            who, n = evacuated(g)
            return S["a_free" if who == "A" else "d_free"], n

        def last_of(name, count):
            return {OWNER[g]: g for g in range(STAGES[name], STAGES[name] + count)}.values()

        def mine(name, count, who):
            return [(n, STAGES[name] + n) for n in range(count) if OWNER[STAGES[name] + n] == who]

        def in_order(eng, name):
            n = [0]

            def then(ins):
                n[0] += 1
                ins.then_inc(S[name], 1)
                eng.wait_ge(S[name], n[0])
            return then

        def at(i):
            return slice(i, i + 1) if isinstance(i, int) else bass.ds(i, 1)

        NORM_XN = (xn_mla, xn_moe, xn_rnn, xn_moe)
        w_ada_v = [w_ada[l].rearrange("(p k) n -> p k n", k=KT) for l in range(2)]
        w_ada_half = w_ada[1].rearrange("(p k) (h n) -> p (k h) n", k=KT, h=2)
        CHUNKS = (0, 1, 3, 4, 2, 5)
        y_rows = ys_dram.rearrange("(i p two) d -> i p (two d)", p=P, two=2)
        out_rows = out[0].rearrange("(i p) d -> i p d", p=P)
        slot_cols = slot_val.rearrange("p j e -> p (j e)")
        tok_cols = slot_tok.rearrange("p j e -> p (j e)")
        NPAIR = NE // 2
        NSTEP = H * TT
        GU = [t.rearrange("p (k n) -> p k n", k=KT) for t in ring_gu]
        DN = [t.rearrange("p (k n) -> p k n", k=FT) for t in ring_dn]

        def gu_rows(l, e):
            return moe_w_gu[l, e].rearrange("(k p) n -> p k n", p=P)

        def dn_rows(l, e):
            return moe_w_dn[l, e].rearrange("(k p) n -> p k n", p=P)

        @block.sync
        def _(sp):
            def load_ada(n):
                ch, hf = divmod(n, 2)
                if counts(n - 1):
                    sp.wait_ge(S["ada_used"], n - 1)
                sp.dma_start(view(ring_gu0, (n % 2) * 4096, 4, D),
                             w_ada_v[0][:, 4 * hf:4 * hf + 4, CHUNKS[ch] * D:(CHUNKS[ch] + 1) * D]
                             ).then_inc(S[f"ada_in{n % 2}"], 16)

            sp.dma_start(c_raw[:, :], c[0].rearrange("(p k) -> p k", k=KT)).then_inc(S["c_in"], 16)
            load_ada(0)
            load_ada(1)
            sp.dma_start(x_tok[:, :, :], x[0].rearrange("(i p) d -> p i d", p=P)).then_inc(S["x_in"], 16)
            load_ada(2)
            load_ada(3)
            sp.dma_start(w_in, mla_w_in[0].rearrange("(k p) n -> p k n", p=P)).then_inc(S["w_in_in"], 16)
            sp.dma_start(w_qb, mla_w_q_b[0].rearrange("(k p) n -> p k n", p=P)).then_inc(S["w_qb_in"], 16)
            for n in range(4, 8):
                load_ada(n)
            sp.wait_ge(S["unit"], STAGES["latT"] + 5)
            sp.dma_start(w_kvb, mla_w_kv_b[0].rearrange("(k p) n -> p k n", p=P)).then_inc(S["w_kvb_in"], 16)
            for n in range(8, 12):
                load_ada(n)
            for l in range(2):
                if l == 0:
                    sp.wait_ge(S["ropeq_done"], 1)
                    sp.dma_start(w_o, mla_w_o[0].rearrange("(k p) n -> p k n", p=P)).then_inc(S["w_o_in"], 16)
                    sp.wait_ge(S["ada_used"], 12)
                    sp.dma_start(GU[0], gu_rows(l, 0)).then_inc(S["gu_in0"], 16)
                else:
                    sp.wait_ge(S["unit"], STAGES["ada1"] + 5)
                    for b in range(NBLK):
                        xcols = slice(D + b * 2 * P, D + (b + 1) * 2 * P)
                        gcols = slice(b * 2 * P, (b + 1) * 2 * P)
                        if b:
                            sp.wait_ge(S["unit"], STAGES[f"xb{b - 1}"] + 2)
                        sp.dma_start(w_xb, rnn_w_in[0][:, xcols].rearrange("(k p) n -> p k n", p=P)
                                     ).then_inc(S["wx_in"], 16)
                        if b:
                            sp.wait_ge(S["unit"], STAGES[f"gate_r{b - 1}"] + 2)
                        sp.dma_start(w_gt, rnn_w_in[0][:, gcols].rearrange("(k p) n -> p k n", p=P)
                                     ).then_inc(S["wg_in"], 16)
                        if b:
                            sp.wait_ge(S["unit"], STAGES[f"rg{b - 1}"] + 8)
                        for m, w in enumerate((rnn_w_rf, rnn_w_if, rnn_w_rb, rnn_w_ib)):
                            sp.dma_start(w_rg[:, 2 * m:2 * m + 2, :], w[0, b].rearrange("(k p) n -> p k n", p=P)
                                         ).then_inc(S["wr_in"], 16)
                        if b == 0:
                            sp.dma_start(w_o, rnn_w_o[0].rearrange("(k p) n -> p k n", p=P)
                                         ).then_inc(S["w_o_in"], 16)
                    sp.wait_ge(S["y_ready"], NBLK)
                    sp.dma_start(GU[0], gu_rows(l, 0)).then_inc(S["gu_in0"], 16)
                sp.wait_ge(S["unit"], STAGES[f"proj{l}"] + 8)
                sp.dma_start(DN[0], dn_rows(l, 0)).then_inc(S["dn_in0"], 16)
                sp.dma_start(GU[1], gu_rows(l, 1)).then_inc(S["gu_in1"], 16)
                sp.wait_ge(S["xn_ready"], 4 * (2 * l + 2))
                sp.dma_start(xn_dram.rearrange("(i p) d -> p i d", p=P), xn_moe).then_inc(S["xn_saved"], 16)
                sp.dma_start(DN[1], dn_rows(l, 1)).then_inc(S["dn_in1"], 16)
                if l == 0:
                    sp.wait_ge(S["unit"], STAGES["logits0"] + 1)
                    for q in range(2):
                        sp.dma_start(stage[:, q, :], w_ada_half[:, q, :]).then_inc(S[f"stage_in{q}"], 16)
                sp.wait_ge(S["table_put"], 8 * 16 * (l + 1))
                sp.dma_start(slot_val[:, :, :], table_dram[l].rearrange("(j p e) o -> p j (e o)", p=P, e=NE)
                             ).then_inc(S["table_in"], 16)

                def pair(it):
                    for q in range(2):
                        n = it * 2 + q - 1 + NE * l
                        sp.wait_ge(S["gu_done"], n)
                        sp.dma_start(GU[q], gu_rows(l, it * 2 + q)).then_inc(S[f"gu_in{q}"], 16)
                        sp.wait_ge(S["dn_done"], n)
                        sp.dma_start(DN[q], dn_rows(l, it * 2 + q)).then_inc(S[f"dn_in{q}"], 16)

                pair(1)
                with sp.Fori(1, NPAIR // 2) as it2:
                    for o in range(2):
                        pair(it2 * 2 + o)
                        if l == 0:
                            sp.wait_ge(S["stage_used"], it2 * 2 + o - 1)
                            sp.dma_start(stage[:, o, :], w_ada_half[:, at(it2 * 2 + o), :]
                                         .rearrange("p o n -> p (o n)")).then_inc(S[f"stage_in{o}"], 16)
                o = OV[l]
                sp.wait_ge(S["slots_ready"], l + 1)
                n_more = sp.value_load(more_i[0:1, 31:32], min_val=0, max_val=MAX_EXTRA)
                sp.wait_ge(S["gu_done"], NE * (l + 1) - 1)
                sp.wait_ge(S["dn_done"], NE * (l + 1) - 1)
                with sp.Fori(0, MAX_EXTRA) as u:
                    with sp.If(n_more > u):
                        e = sp.value_load(more_i[0:1, bass.ds(u + 16, 1)], min_val=0, max_val=NE - 1)
                        sp.wait_ge(o["dn_done"], u + 1)
                        sp.dma_start(GU[0], gu_rows(l, e)).then_inc(o["w_in"], 16)
                        sp.dma_start(DN[0], dn_rows(l, e)).then_inc(o["w_in"], 16)
                sp.wait_ge(S["ov_done"], l + 1)
                for i in range(TT):
                    if counts(TT * l + i - 1):
                        sp.wait_ge(S["y_used"], TT * l + i - 1)
                    sp.dma_start(y_pair[:, i % 2, :], y_rows[i]).then_inc(S[f"y_in{i % 2}"], 16)
            for i in range(TT):
                sp.wait_ge(S["resid_ready"], 3 * TT + i + 1)
                sp.dma_start(out_rows[i], x_tok[:, i, :]).then_inc(S["out_done"], 16)
            sp.wait_ge(S["out_done"], 16 * TT)

        @block.gpsimd
        def _(pool):
            then = in_order(pool, "pool_order")
            g = nc.gpsimd
            g.memset(mrows[:, :], 1.0).then_inc(S["mrow_set"], 1)
            then(g.memset(ident[:, :], 0.0))
            then(g.memset(ones[:, :], 1.0))
            then(g.memset(pick[:, :, :], 0.0))
            then(g.affine_select(out=ident[:, :], in_=ident[:, :], compare_op=ALU.not_equal, fill=1.0, base=0,
                                 pattern=[[-1, P]], channel_multiplier=1))
            then(g.affine_select(out=before[:, :], in_=ones[:, :], compare_op=ALU.is_gt, fill=0.0, base=0,
                                 pattern=[[1, P]], channel_multiplier=-1))
            then(g.affine_select(out=pick[:, :, :], in_=pick[:, :, :], compare_op=ALU.not_equal, fill=1.0, base=0,
                                 pattern=[[-1, 2], [0, P]], channel_multiplier=1))

            def iota(t, pattern, base, cm):
                then(g.iota(t, pattern=pattern, base=base, channel_multiplier=cm,
                            allow_small_or_imprecise_dtypes=True))
            iota(down_e[:, :, :], [[0, TT], [-1, NE]], NE, 0)
            iota(up_e[:, :, :], [[0, TT], [1, NE]], 0, 0)
            iota(down_g[:, :, :], [[0, TT], [-1, NG]], NG, 0)
            iota(tokval[:, :, :], [[2 * P, TT], [1, 2]], 0, 2)
            iota(more_id[:, :], [[1, 3 * NE]], NE, 0)
            for n in range(RH):
                then(g.memset(inv_freq[:, n:n + 1], float(np.float32(10000.0 ** (-n / RH)))))
            then(g.memset(empty[:, :], SKIP))
            g.memset(eps[:, :], EPS).then_inc(S["pool_const"], 1)
            for l in range(2):
                g.dma_start(table_dram[l].rearrange("(p a) o -> p (a o)", p=P), empty[:, :]
                            ).then_inc(S["table_empty"], 16)

            pool.wait_ge(S["table_empty"], 32)
            pool.wait_ge(S["rope_done"], 1)

            def head_inputs(it, hb):
                h = it * 2 + hb
                if counts(it * 2 + hb - 1):
                    pool.wait_ge(S["qkT_made"], it * 2 + hb - 1)
                g.tensor_tensor(qn[:, hb, :, :], q_tok[:, :, at(h), :].rearrange("p i o d -> p i (o d)"),
                                rq[:, :, at(h)].to_broadcast([P, TT, QK]), ALU.mult)
                g.tensor_tensor(kn[:, hb, :, 0:NOPE],
                                kv_tok[:, :, at(h), 0:NOPE].rearrange("p i o d -> p i (o d)"),
                                rk[:, :, at(h)].to_broadcast([P, TT, NOPE]), ALU.mult)
                g.tensor_tensor(kn[:, hb, :, NOPE:QK], k_pe, rk[:, :, at(h)].to_broadcast([P, TT, ROPE]),
                                ALU.mult).then_inc(S["qkn_ready"], 1)

            head_inputs(0, 0)
            head_inputs(0, 1)
            with pool.Fori(1, H // 2) as it:
                head_inputs(it, 0)
                head_inputs(it, 1)

            for l in range(2):
                if l == 1:
                    for b in range(NBLK):
                        gate_s = gate_[b % 2]
                        pool.wait_ge(S["a_free"], evacuated(STAGES[f"gate_r{b}"] + 1)[1])
                        then(g.tensor_tensor(gtmp, gate_s, gate_s, ALU.mult))
                        then(g.tensor_scalar(gtmp, gtmp, 0.044715, 1.0, ALU.mult, ALU.add))
                        g.tensor_tensor(gtmp, gtmp, gate_s, ALU.mult).then_inc(S["gz_ready"], 1)
                        pool.wait_ge(S["gs_ready"], b + 1)
                        then(g.tensor_tensor(gate_s, gate_s, gtmp, ALU.mult))
                        pool.sem_inc(S["gelu_ready"], 1)
                pool.wait_ge(S["table_empty"], 32)
                pool.wait_ge(S["xn_saved"], 16 * (l + 1))
                pool.wait_ge(S["unit"], STAGES[f"norm{2 * l + 1}"] + 8)
                g.memset(xg[:, :, :], 0.0).then_inc(S["xg_clear"], 1)
                if l == 0:
                    g.memset(acc1_flat, 0.0).then_inc(S["acc1_zero"], 1)
                    pool.wait_ge(S["acc1_zero"], 1)
                    g.dma_start(acc1_flat[0:1, :], b_ada[1:2, :]).then_inc(S["acc1_bias"], 16)
                pool.wait_ge(S["dest_ready"], l + 1)
                for i in range(TT):
                    for k in range(2):
                        g.indirect_dma_start(
                            table_dram[l], bass.IndirectOffsetOnAxis(ap=dest[:, i, k:k + 1], axis=0),
                            tokval[:, i, k:k + 1], None, bounds_check=SEQ * NE - 1,
                            oob_is_err=False).then_inc(S["table_put"], 16)
                pool.wait_ge(S["xg_clear"], l + 1)
                pool.wait_ge(S["slots_ready"], l + 1)

                def gather(e, q):
                    if counts(e + NE * l - 1):
                        pool.wait_ge(S["xT_made"], e + NE * l - 1)
                    g.tensor_copy(idx_in[:, q:q + 1], tok_cols[:, at(e)]).then_inc(S["idx_in_set"], 1)
                    pool.wait_ge(S["idx_in_set"], e + NE * l + 1)
                    pool.sem_inc(S["pool_step"], 1)
                    g.indirect_dma_start(xg[:, q, :], None, xn_dram,
                                         bass.IndirectOffsetOnAxis(ap=idx_in[:, q:q + 1], axis=0),
                                         bounds_check=SEQ - 1, oob_is_err=False).then_inc(S[f"gathered{q}"], 16)

                def scatter(e, q, pair_no):
                    if counts((pair_no + NPAIR * l) * 16):
                        pool.wait_ge(S[f"scattered{q}"], (pair_no + NPAIR * l) * 16)
                    g.tensor_copy(idx_out[:, q:q + 1], slot_cols[:, at(e)]).then_inc(S["idx_out_set"], 1)
                    pool.wait_ge(S["idx_out_set"], e + NE * l + 1)
                    pool.wait_ge(S["yo_a"], e + NE * l + 1)
                    pool.wait_ge(S["yo_d"], e + NE * l + 1)
                    pool.sem_inc(S["pool_step"], 1)
                    g.indirect_dma_start(ys_dram, bass.IndirectOffsetOnAxis(ap=idx_out[:, q:q + 1], axis=0),
                                         yo[:, q, :], None, bounds_check=2 * SEQ - 1,
                                         oob_is_err=False).then_inc(S[f"scattered{q}"], 16)

                gather(0, 0)
                gather(1, 1)
                gather(2, 0)
                gather(3, 1)
                with pool.Fori(1, NPAIR - 1) as it:
                    gather(it * 2 + 2, 0)
                    scatter(it * 2 - 2, 0, it - 1)
                    gather(it * 2 + 3, 1)
                    scatter(it * 2 - 1, 1, it - 1)
                o = OV[l]

                def gather_more(u):
                    col = pool.value_load(more_i[0:1, bass.ds(u, 1)], min_val=0, max_val=4 * NE - 1)
                    g.tensor_copy(idx_in[:, 2:3], tok_cols[:, bass.ds(col, 1)]).then_inc(o["idx"], 1)
                    pool.wait_ge(o["idx"], u * 2 + 1)
                    pool.sem_inc(S["pool_step"], 1)
                    g.indirect_dma_start(xg[:, 0, :], None, xn_dram,
                                         bass.IndirectOffsetOnAxis(ap=idx_in[:, 2:3], axis=0),
                                         bounds_check=SEQ - 1, oob_is_err=False).then_inc(o["gathered"], 16)

                for e in range(NE - 4, NE):
                    if e == NE - 2:
                        pool.wait_ge(S["xT_made"], NE * (l + 1))
                        gather_more(0)
                    scatter(e, e % 2, e // 2)
                n_more = pool.value_load(more_i[0:1, 31:32], min_val=0, max_val=MAX_EXTRA)
                with pool.Fori(0, MAX_EXTRA) as u:
                    with pool.If(n_more > u):
                        col = pool.value_load(more_i[0:1, bass.ds(u, 1)], min_val=0, max_val=4 * NE - 1)
                        g.tensor_copy(idx_out[:, 2:3], slot_cols[:, bass.ds(col, 1)]).then_inc(o["idx"], 1)
                        pool.wait_ge(o["idx"], u * 2 + 2)
                        pool.wait_ge(o["yo_a"], u + 1)
                        pool.wait_ge(o["yo_d"], u + 1)
                        pool.sem_inc(S["pool_step"], 1)
                        g.indirect_dma_start(ys_dram, bass.IndirectOffsetOnAxis(ap=idx_out[:, 2:3], axis=0),
                                             yo[:, 0, :], None, bounds_check=2 * SEQ - 1,
                                             oob_is_err=False).then_inc(o["scattered"], 16)
                        pool.wait_ge(o["scattered"], u * 16 + 16)
                        pool.wait_ge(o["xT_made"], u + 1)
                        gather_more(u + 1)
                        pool.wait_ge(o["gathered"], u * 16 + 32)
                pool.wait_ge(o["gathered"], 16)
                pool.wait_ge(S["scattered0"], 16 * NPAIR * (l + 1))
                pool.wait_ge(S["scattered1"], 16 * NPAIR * (l + 1))
                g.memset(tick[:, :], 0.0).then_inc(S["ov_done"], 1)

        @block.tensor
        def _(pe):
            mm, tr = nc.tensor.matmul, nc.tensor.transpose

            pe.wait_ge(S["pool_const"], 1)
            pe.wait_ge(S["rows_in"], 16 * 10)
            pe.wait_ge(S["brow_in"], 32)
            pe.wait_ge(S["mrow_in"], 16 * 4)
            g = STAGES["setup"]
            tr(bank(g)[:, 0:NVROW], vrows[:, :], ident[0:NVROW, 0:NVROW]).then_inc(S["unit"], 1)
            tr(bank(g + 1)[:, 0:48], brows[:, :], ident[0:48, 0:48]).then_inc(S["unit"], 1)
            tr(bank(g + 2)[:, 0:7], mrows[:, :], ident[0:7, 0:7]).then_inc(S["unit"], 1)

            def sum_columns(g, acc, dst0):
                for k in range(KT):
                    last = mm(bank(g)[:, dst0 + k:dst0 + k + 1], acc[:, k * P:(k + 1) * P], ones[:, 0:1],
                              start=True, stop=True)
                return last

            def sum_rows(g, acc, r, hf):
                half = acc[:, hf * HALF:(hf + 1) * HALF]
                if r is None:
                    return mm(bank(g), ones[:, :], half, start=True, stop=True)
                mm(bank(g), ones[:, :], half, start=True, stop=False)
                return mm(bank(g), pick[:, r, :], gate_bias[:, hf * HALF:(hf + 1) * HALF], start=False, stop=True)

            for n in range(2):
                g = STAGES["cols0"] + n
                pe.wait_ge(S["ada_used"], 2 * (n + 1))
                sum_columns(g, gate_bc[:, n, :], 0).then_inc(S["unit"], 1)

            def norm_transposes(u):
                xn = NORM_XN[u]
                for k in range(KT):
                    g = STAGES[f"norm{u}"] + k
                    if g >= 8:
                        pe.wait_ge(*emptied(g - 8))
                    for i in range(TT):
                        if k == 0:
                            pe.wait_ge(S["xn_ready"], 4 * u + i + 1)
                        last = tr(bank(g)[:, i * P:(i + 1) * P], xn[:, i, k * P:(k + 1) * P], ident[:, :])
                    last.then_inc(S["unit"], 1)

            def project_out(l, src):
                for i in range(TT):
                    for hf in range(2):
                        g = STAGES[f"proj{l}"] + 2 * i + hf
                        if g >= 8:
                            pe.wait_ge(*emptied(g - 8))
                        for k in range(KT):
                            last = mm(bank(g), src[:, k, i * P:(i + 1) * P], w_o[:, k, hf * HALF:(hf + 1) * HALF],
                                      start=(k == 0), stop=(k == KT - 1))
                        last.then_inc(S["unit"], 1)

            norm_transposes(0)
            pe.wait_ge(S["w_in_in"], 16)
            for last_unit in last_of("norm0", 8):
                pe.wait_ge(*emptied(last_unit))
            for i in range(TT):
                for hf, width in enumerate((HALF, LAT - HALF)):
                    g = STAGES["lat"] + 2 * i + hf
                    if g >= 8:
                        pe.wait_ge(*emptied(g - 8))
                    for k in range(KT):
                        last = mm(bank(g)[:, 0:width], hT[:, k, i * P:(i + 1) * P],
                                  w_in[:, k, hf * HALF:hf * HALF + width], start=(k == 0), stop=(k == KT - 1))
                    last.then_inc(S["unit"], 1)
            pe.wait_ge(S["lat_scaled"], 1)
            for ch in range(5):
                g = STAGES["latT"] + ch
                if g >= 8:
                    pe.wait_ge(*emptied(g - 8))
                for i in range(TT):
                    last = tr(bank(g)[:, i * P:(i + 1) * P], lat[:, i, ch * P:(ch + 1) * P], ident[:, :])
                last.then_inc(S["unit"], 1)
            pe.wait_ge(S["w_qb_in"], 16)
            for last_unit in last_of("latT", 5):
                pe.wait_ge(*emptied(last_unit))
            for i in range(TT):
                for n in range(3):
                    g = STAGES["q"] + 3 * i + n
                    if g >= 8:
                        pe.wait_ge(*emptied(g - 8))
                    for k in range(3):
                        last = mm(bank(g), latT[:, k, i * P:(i + 1) * P], w_qb[:, k, n * HALF:(n + 1) * HALF],
                                  start=(k == 0), stop=(k == 2))
                    last.then_inc(S["unit"], 1)
            for n in range(2):
                g = STAGES["ffncols0"] + n
                if g >= 8:
                    pe.wait_ge(*emptied(g - 8))
                pe.wait_ge(S["ada_used"], 2 * (n + 3))
                sum_columns(g, gate_bc[:, n, :], 0).then_inc(S["unit"], 1)
            pe.wait_ge(S["w_kvb_in"], 16)
            for i in range(TT):
                for n in range(4):
                    g = STAGES["kv"] + 4 * i + n
                    if g >= 8:
                        pe.wait_ge(*emptied(g - 8))
                    for k in range(2):
                        last = mm(bank(g), latT[:, 3 + k, i * P:(i + 1) * P], w_kvb[:, k, n * HALF:(n + 1) * HALF],
                                  start=(k == 0), stop=(k == 1))
                    last.then_inc(S["unit"], 1)
            for n in range(4):
                g = STAGES["gate0"] + n
                if g >= 8:
                    pe.wait_ge(*emptied(g - 8))
                pe.wait_ge(S["ada_used"], 2 * (n // 2 + 5))
                sum_rows(g, gate_bc[:, n // 2, :], n // 2, n % 2).then_inc(S["unit"], 1)

            for last_unit in last_of("kv", 16):
                pe.wait_ge(*emptied(last_unit))
            for last_unit in last_of("gate0", 4):
                pe.wait_ge(*emptied(last_unit))

            def head_transposes(h, hb):
                pe.wait_ge(S["qkn_ready"], h + 1)
                if counts(h):
                    pe.wait_ge(S["qT_ready"], h)
                if counts(h):
                    pe.wait_ge(S["kT_ready"], h)
                for b, src in ((0, qn), (1, kn)):
                    for i in range(TT):
                        last = tr(ps[0:QK, b, i * P:(i + 1) * P], src[:, hb, i, :], ident[:, :])
                last.then_inc(S["qkT_made"], 1)

            def head_step(it, p, last_pair=False, tail=False):
                s = it * 8 + p
                h = it * 2 + p // 4
                hb, qt = p // 4, p % 4
                if not tail:
                    if qt == 0:
                        pe.wait_ge(S["qT_ready"], h + 1)
                        pe.wait_ge(S["kT_ready"], h + 1)
                    if counts(s - 3):
                        pe.wait_ge(S["p_ready"], s - 3)
                    mm(ps[:, 2 + qt, :], qT[0:QK, hb, qt * P:(qt + 1) * P], kT[0:QK, hb, :],
                       start=True, stop=True).then_inc(S["s_ready"], 1)
                    if qt == 2 and not (last_pair and p == 6):
                        head_transposes(h + 1, (hb + 1) % 2)
                if not (isinstance(s, int) and (s < 2 or s >= NSTEP + 2)):
                    pe.wait_ge(S["p_ready"], s - 1)
                    if p % 2 == 1:
                        pe.wait_ge(S["pT_a"], (it * 4 + (p - 3) // 2) + 1)
                    else:
                        if counts((it * 4 + (p - 4) // 2) + 1):
                            pe.wait_ge(S["pT_d"], (it * 4 + (p - 4) // 2) + 1)
                    for kt in range(TT):
                        last = tr(ps[:, 6, kt * P:(kt + 1) * P], probs[:, p % 2, kt * P:(kt + 1) * P], ident[:, :])
                    last.then_inc(S["pT_made"], 1)
                if not (isinstance(s, int) and s < 3):
                    hv, qv = it * 2 + (p - 3) // 4, (p - 3) % 4
                    if isinstance(s, int) and s >= NSTEP + 2:
                        if p % 2 == 1:
                            pe.wait_ge(S["pT_a"], (it * 4 + (p - 3) // 2) + 1)
                        else:
                            if counts((it * 4 + (p - 4) // 2) + 1):
                                pe.wait_ge(S["pT_d"], (it * 4 + (p - 4) // 2) + 1)
                    if qv == 0:
                        if counts(hv):
                            pe.wait_ge(S["o_done"], hv)
                    for kt in range(TT):
                        last = mm(ps[:, 7, qv * VH:(qv + 1) * VH], probsT[:, (p - 3) % 2, kt, :],
                                  kv_tok[:, kt, at(hv), NOPE:NOPE + VH].rearrange("p o d -> p (o d)"),
                                  start=(kt == 0), stop=(kt == TT - 1))
                    last.then_inc(S["pv_done"], 1)

            head_transposes(0, 0)
            for p in range(8):
                head_step(0, p)
            with pe.Fori(1, H // 2 - 1) as it:
                for p in range(8):
                    head_step(it, p)
            for p in range(8):
                head_step(H // 2 - 1, p, last_pair=True)
            for p in range(3):
                head_step(H // 2, p, tail=True)

            pe.wait_ge(S["o_done"], H)
            for k in range(KT):
                g = STAGES["oT"] + k
                if g >= 8:
                    pe.wait_ge(*emptied(g - 8))
                for i in range(TT):
                    last = tr(bank(g)[:, i * P:(i + 1) * P], o_tok[:, i, k * P:(k + 1) * P], ident[:, :])
                last.then_inc(S["unit"], 1)
            pe.wait_ge(S["w_o_in"], 16)
            for last_unit in last_of("oT", 8):
                pe.wait_ge(*emptied(last_unit))
            project_out(0, oT)

            for l in range(2):
                if l == 1:
                    norm_transposes(2)
                    for last_unit in last_of("norm2", 8):
                        pe.wait_ge(*emptied(last_unit))

                    def channels(name, b, w, w_sem):
                        pe.wait_ge(S[w_sem], 16 * (b + 1))
                        for m in range(2):
                            g = STAGES[f"{name}{b}"] + m
                            if g >= 8:
                                pe.wait_ge(*emptied(g - 8))
                            for k in range(KT):
                                last = mm(bank(g), w[:, k, m * P:(m + 1) * P], hT[:, k, :],
                                          start=(k == 0), stop=(k == KT - 1))
                            last.then_inc(S["unit"], 1)

                    channels("xb", 0, w_xb, "wx_in")
                    for b in range(NBLK):
                        channels("gate_r", b, w_gt, "wg_in")
                        if b < NBLK - 1:
                            channels("xb", b + 1, w_xb, "wx_in")
                        pe.wait_ge(S["wr_in"], 64 * (b + 1))
                        pe.wait_ge(S["xc_ready"], b + 1)
                        for n in range(8):
                            mat, m = divmod(n, 2)
                            g = STAGES[f"rg{b}"] + n
                            if g >= 8:
                                pe.wait_ge(*emptied(g - 8))
                            for k in range(2):
                                last = mm(bank(g), w_rg[:, 2 * mat + k, m * P:(m + 1) * P], xc_[b % 2][:, k, :],
                                          start=(k == 0), stop=(k == 1))
                            last.then_inc(S["unit"], 1)
                    ready = 2 * (NBLK - 1)
                    pe.wait_ge(S["w_o_in"], 32)
                    pe.wait_ge(S["y_ready"], NBLK - 1)
                    for ks in (range(ready), range(ready, KT)):
                        if ks[0]:
                            pe.wait_ge(S["y_ready"], NBLK)
                        for n in range(2 * TT):
                            i, hf = divmod(n, 2)
                            g = STAGES["proj1"] + n
                            if ks[0] == 0:
                                pe.wait_ge(*emptied(g - 8))
                            for k in ks:
                                last = mm(bank(g), yT[:, k, i * P:(i + 1) * P], w_o[:, k, hf * HALF:(hf + 1) * HALF],
                                          start=(k == 0), stop=(k == KT - 1))
                            if ks[0]:
                                last.then_inc(S["unit"], 1)

                norm_transposes(2 * l + 1)
                for last_unit in last_of(f"norm{2 * l + 1}", 8):
                    pe.wait_ge(*emptied(last_unit))
                pe.wait_ge(S["router_in"], 16)
                g = STAGES[f"logits{l}"]
                if g >= 8:
                    pe.wait_ge(*emptied(g - 8))
                for i in range(TT):
                    for k in range(KT):
                        last = mm(bank(g)[:, i * NE:(i + 1) * NE], hT[:, k, i * P:(i + 1) * P], router_w[:, k, :],
                                  start=(k == 0), stop=(k == KT - 1))
                last.then_inc(S["unit"], 1)
                pe.wait_ge(S["chosen_ready"], l + 1)
                g = STAGES[f"rank{l}"]
                if g >= 8:
                    pe.wait_ge(*emptied(g - 8))
                for i in range(TT):
                    for j in range(i + 1):
                        last = mm(bank(g)[:, i * NE:(i + 1) * NE], (before if j == i else ones)[:, :],
                                  chosen[:, j, :], start=(j == 0), stop=(j == i))
                last.then_inc(S["unit"], 1)
                if g + 1 >= 8:
                    pe.wait_ge(*emptied(g + 1 - 8))
                for j in range(TT):
                    last = mm(bank(g + 1)[:, 0:NE], ones[:, :], chosen[:, j, :], start=(j == 0), stop=(j == TT - 1))
                last.then_inc(S["unit"], 1)

                for last_unit in last_of(f"norm{2 * l + 1}", 8):
                    pe.wait_ge(*emptied(last_unit))
                for last_unit in last_of(f"logits{l}", 1):
                    pe.wait_ge(*emptied(last_unit))
                for last_unit in last_of(f"rank{l}", 2):
                    pe.wait_ge(*emptied(last_unit))
                base = NE * l

                def rows_transposed(rows):
                    for k in range(KT):
                        last = tr(ps[:, k // 4, (k % 4) * P:(k % 4 + 1) * P], rows[:, k * P:(k + 1) * P], ident[:, :])
                    return last

                def gate_up(w):
                    for k in range(KT):
                        for hf in range(2):
                            last = mm(ps[:, 2 + hf, :], xgT[:, k, :], w[:, k, hf * HALF:(hf + 1) * HALF],
                                      start=(k == 0), stop=(k == KT - 1))
                    return last

                def hidden_transposed():
                    for f in range(FT):
                        last = tr(ps[:, 4, f * P:(f + 1) * P], hmid[:, f * P:(f + 1) * P], ident[:, :])
                    return last

                def down(w):
                    for f in range(FT):
                        for hf in range(2):
                            last = mm(ps[:, 5 + hf, :], hmidT[:, f, :], w[:, f, hf * HALF:(hf + 1) * HALF],
                                      start=(f == 0), stop=(f == FT - 1))
                    return last

                def rows(e, q, pair_no):
                    pe.wait_ge(S[f"gathered{q}"], (pair_no + NPAIR * l + 1) * 16)
                    rows_transposed(xg[:, q, :]).then_inc(S["xT_made"], 1)

                def expert(it, q, first=False, last=False):
                    e = it * 2 + q + base
                    pe.wait_ge(S["xT_a"], e + 1)
                    pe.wait_ge(S["xT_d"], e + 1)
                    pe.wait_ge(S[f"gu_in{q}"], (it + NPAIR * l + 1) * 16)
                    if counts(e):
                        pe.wait_ge(S["hmid_ready"], e)
                    gate_up(GU[q]).then_inc(S["gu_done"], 1)
                    if not first:
                        hidden_transposed().then_inc(S["hT_made"], 1)
                    if not last:
                        rows(e + 1, 1 - q, it + q)
                    if not first:
                        expert_down(it if q else it - 1, 1 - q, e - 1)

                def expert_down(pair_no, q, e):
                    pe.wait_ge(S["hmidT_ready"], e + 1)
                    pe.wait_ge(S[f"dn_in{q}"], (pair_no + NPAIR * l + 1) * 16)
                    if counts(e):
                        pe.wait_ge(S["yo_a"], e)
                    if counts(e):
                        pe.wait_ge(S["yo_d"], e)
                    down(DN[q]).then_inc(S["dn_done"], 1)

                pe.sem_inc(OV[l]["dn_done"], 1)
                rows(0, 0, 0)
                expert(0, 0, first=True)
                expert(0, 1)
                with pe.Fori(1, NPAIR - 1) as it:
                    expert(it, 0)
                    expert(it, 1)
                expert(NPAIR - 1, 0)
                expert(NPAIR - 1, 1, last=True)
                pe.wait_ge(S["hmid_ready"], base + NE)
                hidden_transposed().then_inc(S["hT_made"], 1)
                expert_down(NPAIR - 1, 1, base + NE - 1)
                pe.wait_ge(S["yo_a"], base + NE)
                pe.wait_ge(S["yo_d"], base + NE)
                o = OV[l]
                n_more = pe.value_load(more_i[0:1, 31:32], min_val=0, max_val=MAX_EXTRA)
                with pe.Fori(0, MAX_EXTRA) as u:
                    with pe.If(n_more > u):
                        pe.wait_ge(o["gathered"], u * 16 + 16)
                        rows_transposed(xg[:, 0, :]).then_inc(o["xT_made"], 1)
                        pe.wait_ge(o["xT_ready"], u + 1)
                        pe.wait_ge(o["w_in"], u * 32 + 32)
                        gate_up(GU[0]).then_inc(o["gu_done"], 1)
                        pe.wait_ge(o["hmid"], u + 1)
                        hidden_transposed().then_inc(o["hT_made"], 1)
                        pe.wait_ge(o["hmidT"], u + 1)
                        down(DN[0]).then_inc(o["dn_done"], 1)
                        pe.wait_ge(o["yo_a"], u + 1)
                        pe.wait_ge(o["yo_d"], u + 1)
                if l == 0:
                    g = STAGES["ada1"]
                    pe.wait_ge(S["stage_used"], NPAIR)
                    if g >= 8:
                        pe.wait_ge(*emptied(g - 8))
                    for n, ch in enumerate(CHUNKS[0:4]):
                        last = sum_columns(g, acc1_flat[:, ch * D:(ch + 1) * D], n * KT)
                    last.then_inc(S["unit"], 1)
                    for n in range(4):
                        if g + 1 + n >= 8:
                            pe.wait_ge(*emptied(g + 1 + n - 8))
                        ch = CHUNKS[4 + n // 2]
                        sum_rows(g + 1 + n, acc1_flat[:, ch * D:(ch + 1) * D], None, n % 2).then_inc(S["unit"], 1)

        @block.scalar
        def _(act):
            then = in_order(act, "act_order")
            A = nc.scalar.activation

            for name, src in (("norm_mix", norm_mix), ("norm_ffn", norm_ffn), ("conv_w", rnn_conv_w[0]),
                              ("conv_b", rnn_conv_b), ("lam_f", rnn_lam_f), ("b_rf", rnn_b_rf), ("b_if", rnn_b_if),
                              ("lam_b", rnn_lam_b), ("b_rb", rnn_b_rb), ("b_ib", rnn_b_ib)):
                r0, rows = VROW[name], VCOUNT[name]
                act.dma_start(vrows[r0:r0 + rows, :], src.rearrange("a (k p) -> (a k) p", p=P)
                              ).then_inc(S["rows_in"], 16)
            act.dma_start(pos_i[:, :], positions[0].rearrange("(i p) -> p i", p=P), allow_slow_non_contiguous=True).then_inc(S["misc_in"], 16)
            for n, src in enumerate((mla_q_norm, mla_k_norm)):
                act.dma_start(ropeg[:, n, :], src[0, NOPE:QK].partition_broadcast(P)).then_inc(S["misc_in"], 16)
            act.dma_start(rbias[:, :], router_bias.partition_broadcast(P)).then_inc(S["misc_in"], 16)
            act.dma_start(brows[:, :], b_ada[0].rearrange("(k p) -> k p", p=P)).then_inc(S["brow_in"], 16)
            act.dma_start(gate_bias[:, :], b_ada[0].rearrange("(s n) -> s n", n=D)[2:6:3, :]
                          ).then_inc(S["brow_in"], 16)
            act.wait_ge(S["c_in"], 16)
            A(c_act[:, :], c_raw[:, :], ACT.Silu).then_inc(S["c_ready"], 1)
            act.wait_ge(S["mrow_set"], 1)
            act.dma_start(mrows[0:3, :], mla_q_a_norm[0].rearrange("(k p) -> k p", p=P)).then_inc(S["mrow_in"], 16)
            act.dma_start(mrows[3:5, :], mla_kv_a_norm[0].rearrange("(k p) -> k p", p=P)).then_inc(S["mrow_in"], 16)
            act.dma_start(mrows[5:6, 0:NOPE], mla_q_norm[0:1, 0:NOPE]).then_inc(S["mrow_in"], 16)
            act.dma_start(mrows[6:7, 0:NOPE], mla_k_norm[0:1, 0:NOPE]).then_inc(S["mrow_in"], 16)
            act.dma_start(router_w[:, :, :], w_router.rearrange("(k p) n -> p k n", p=P)).then_inc(S["router_in"], 16)

            act.wait_ge(S["pool_const"], 1)

            def rms_stats(u):
                xn = NORM_XN[u]
                for i in range(TT):
                    if u == 0:
                        act.wait_ge(S["x_in"], 16)
                    else:
                        act.wait_ge(S["resid_ready"], 4 * (u - 1) + i + 1)
                    last = A(xn[:, i, :], x_tok[:, i, :], ACT.Square, accum_out=ss[:, i:i + 1])
                then(last)
                A(std[:, :], ss[:, :], ACT.Sqrt, bias=eps[:, :], scale=1.0 / D).then_inc(S["ss_ready"], 1)

            def modulated(u):
                act.wait_ge(S["mod_ready"], u + 1)
                for k, g in mine(f"norm{u}", KT, "A"):
                    act.wait_ge(S["unit"], g + 1)
                    A(hT[:, k, :], bank(g), ACT.Identity, scale=scale_col[:, u, k:k + 1],
                      bias=shift_col[:, u, k:k + 1]).then_inc(S["a_free"], 1)

            rms_stats(0)
            modulated(0)
            for n, g in mine("lat", 8, "A"):
                act.wait_ge(S["unit"], g + 1)
                i = n // 2
                A(lat[:, i, 0:HALF], bank(g), ACT.Copy).then_inc(S["a_free"], 1)
                act.wait_ge(*emptied(g))
                act.wait_ge(*emptied(g + 1))
                then(A(lat_sq_tmp, lat[:, i, 0:QL], ACT.Square, accum_out=lat_ss[:, 0, i:i + 1]))
                then(A(lat_sq_tmp[:, 0:KVL], lat[:, i, QL:QL + KVL], ACT.Square,
                       accum_out=lat_ss[:, 1, i:i + 1]))
            A(lat_r[:, 0, :], lat_ss[:, 0, :], ACT.Sqrt, bias=eps[:, :], scale=1.0 / QL)
            A(lat_r[:, 1, :], lat_ss[:, 1, :], ACT.Sqrt, bias=eps[:, :], scale=1.0 / KVL).then_inc(S["lat_stat"], 1)
            act.wait_ge(S["angle_ready"], 1)
            A(trig[:, 3:5, :, :], trig[:, 3:5, :, :], ACT.Sin).then_inc(S["trig_ready"], 1)
            act.wait_ge(S["lam_abs"], 1)
            A(lam_t[:, 1, :], lam_t[:, 0, :], ACT.Exp, scale=-1.0).then_inc(S["lam_exp"], 1)
            for ch, g in mine("latT", 5, "A"):
                act.wait_ge(S["unit"], g + 1)
                A(latT[:, ch, :], bank(g), ACT.Copy, scale=mcols[:, ch:ch + 1]).then_inc(S["a_free"], 1)

            def head_squares(n, out, in_):
                if counts(n - 1):
                    act.wait_ge(S["sq_used"], n - 1)
                A(out, in_, ACT.Square).then_inc(S["sq_ready"], 1)

            act.wait_ge(S["unit"], STAGES["lat"] + 8)
            for n, g in mine("q", 12, "A"):
                act.wait_ge(S["unit"], g + 1)
                A(q_flat[:, n * HALF:(n + 1) * HALF], bank(g), ACT.Copy).then_inc(S["a_free"], 1)
                if n % 3 == 2:
                    i = n // 3
                    act.wait_ge(S["a_free"], evacuated(g)[1])
                    head_squares(i, sq_tmp[:, i % 2, :], q_flat[:, i * H * QK:(i + 1) * H * QK])
            act.wait_ge(S["unit"], STAGES["q"] + 12)
            for n, g in mine("kv", 16, "A"):
                act.wait_ge(S["unit"], g + 1)
                A(kv_flat[:, n * HALF:(n + 1) * HALF], bank(g), ACT.Copy).then_inc(S["a_free"], 1)
                if n % 4 == 3:
                    i = n // 4
                    act.wait_ge(S["a_free"], evacuated(g)[1])
                    head_squares(TT + i, sq_tmp[:, i % 2, 0:H * NOPE].rearrange("p (h d) -> p h d", h=H),
                                 kv_tok[:, i, :, 0:NOPE])
            act.wait_ge(S["qk_var"], 1)
            A(rq, rq, ACT.Sqrt, bias=eps[:, :], scale=1.0 / QK)
            A(rk, rk, ACT.Sqrt, bias=eps[:, :], scale=1.0 / QK).then_inc(S["qk_std"], 1)

            def q_out(h, hb):
                act.wait_ge(S["qkT_made"], h + 1)
                A(qT[0:QK, hb, :], ps[0:QK, 0, :], ACT.Copy, scale=q_gain[0:QK, :]).then_inc(S["qT_ready"], 1)

            def head_step(it, p, last_pair=False, tail=False):
                s = it * 8 + p
                if not tail:
                    act.wait_ge(S["nmax_ready"], s + 1)
                    if counts(s - 1):
                        act.wait_ge(S["pT_made"], s - 1)
                    A(probs[:, p % 2, :], ps[:, 2 + p % 4, :], ACT.Exp, bias=nmax[:, p % 4:p % 4 + 1],
                      accum_out=rsum[:, p // 4, p % 4:p % 4 + 1]).then_inc(S["p_ready"], 1)
                if p % 2 == 0 and not (isinstance(s, int) and (s < 2 or s >= NSTEP + 2)):
                    act.wait_ge(S["pT_made"], s - 1)
                    if counts(s - 3):
                        act.wait_ge(S["pv_done"], s - 3)
                    A(probsT[:, 0, :, :], ps[:, 6, :].rearrange("p (a b) -> p a b", a=TT), ACT.Copy
                      ).then_inc(S["pT_a"], 1)
                if p % 4 == 2 and not tail and not (last_pair and p == 6):
                    q_out(it * 2 + p // 4 + 1, (p // 4 + 1) % 2)

            act.wait_ge(S["cols_set"], 1)
            q_out(0, 0)
            for p in range(8):
                head_step(0, p)
            with act.Fori(1, H // 2 - 1) as it:
                for p in range(8):
                    head_step(it, p)
            for p in range(8):
                head_step(H // 2 - 1, p, last_pair=True)
            head_step(H // 2, 0, tail=True)
            for k, g in mine("oT", 8, "A"):
                act.wait_ge(S["unit"], g + 1)
                A(oT[:, k, :], bank(g), ACT.Copy).then_inc(S["a_free"], 1)

            for l in range(2):
                if l == 1:
                    rms_stats(2)
                    modulated(2)
                    for b in range(NBLK):
                        if counts(b - 1):
                            act.wait_ge(S["y_ready"], b - 1)
                        for m, g in mine(f"gate_r{b}", 2, "A"):
                            act.wait_ge(S["unit"], g + 1)
                            A(gate_[b % 2][:, m, :], bank(g), ACT.Copy).then_inc(S["a_free"], 1)
                        act.wait_ge(S["gz_ready"], b + 1)
                        A(gtmp, gtmp, ACT.Sigmoid, scale=GELU_SCALE).then_inc(S["gs_ready"], 1)
                        if counts(b):
                            act.wait_ge(S["y_ready"], b)
                        for n in range(8):
                            mat, m = divmod(n, 2)
                            g = STAGES[f"rg{b}"] + n
                            act.wait_ge(S["unit"], g + 1)
                            col = VROW[("b_rf", "b_if", "b_rb", "b_ib")[mat]] + 2 * b + m
                            dst = (r_s, i_s)[mat % 2][:, (mat // 2) * 2 + m, :]
                            last = A(dst, bank(g), ACT.Sigmoid, bias=vcols[:, col:col + 1])
                            last.then_inc(S["a_free"], 1)
                        act.wait_ge(S["a_free"], evacuated(STAGES[f"rg{b}"] + 7)[1])
                        for dr in range(2):
                            for m in range(2):
                                last = A(t_s[:, dr * 2 + m, :], r_s[:, dr * 2 + m, :], ACT.Tanh,
                                         scale=lam_c[:, dr, 2 * b + m:2 * b + m + 1])
                        last.then_inc(S["t_ready"], 1)
                        act.wait_ge(S["t_ready"], b + 1)
                        act.wait_ge(S["rc_ready"], b + 1)
                        A(t_s, t_s, ACT.Sqrt).then_inc(S["st_ready"], 1)
                rms_stats(2 * l + 1)
                modulated(2 * l + 1)
                (_, g), = mine(f"logits{l}", 1, "A")
                act.wait_ge(S["unit"], g + 1)
                A(scores.rearrange("p i e -> p (i e)"), bank(g)[:, 0:TT * NE], ACT.Sigmoid).then_inc(S["a_free"], 1)

                base = NE * l
                u = 2 * l + 1

                def rows_out(e):
                    act.wait_ge(S["xT_made"], e + 1)
                    for k in range(4):
                        last = A(xgT[:, k, :], ps[:, 0, k * P:(k + 1) * P], ACT.Identity,
                                 scale=scale_col[:, u, k:k + 1], bias=shift_col[:, u, k:k + 1])
                    last.then_inc(S["xT_a"], 1)

                def hidden_out(e):
                    act.wait_ge(S["hT_made"], e + 1)
                    A(hmidT, ps[:, 4, :].rearrange("p (a b) -> p a b", a=FT), ACT.Copy
                      ).then_inc(S["hmidT_ready"], 1)

                def down_out(pair_no, q, e):
                    if counts((pair_no + NPAIR * l) * 16):
                        act.wait_ge(S[f"scattered{q}"], (pair_no + NPAIR * l) * 16)
                    act.wait_ge(S["dn_done"], e + 1)
                    A(yo[:, q, 0:HALF], ps[:, 5, :], ACT.Copy).then_inc(S["yo_a"], 1)

                def expert(it, q, first=False, last=False):
                    e = it * 2 + q + base
                    if not first:
                        hidden_out(e - 1)
                    act.wait_ge(S["gu_done"], e + 1)
                    if counts(e):
                        act.wait_ge(S["hmid_ready"], e)
                    A(hsil, ps[:, 2, :], ACT.Silu).then_inc(S["sil_ready"], 1)
                    if not last:
                        rows_out(e + 1)
                    if not first:
                        down_out(it if q else it - 1, 1 - q, e - 1)

                rows_out(base)
                expert(0, 0, first=True)
                expert(0, 1)
                with act.Fori(1, NPAIR - 1) as it:
                    expert(it, 0)
                    expert(it, 1)
                expert(NPAIR - 1, 0)
                expert(NPAIR - 1, 1, last=True)
                hidden_out(base + NE - 1)
                down_out(NPAIR - 1, 1, base + NE - 1)
                o = OV[l]
                act.wait_ge(S["slots_ready"], l + 1)
                act.wait_ge(S["scattered0"], 16 * NPAIR * (l + 1))
                n_more = act.value_load(more_i[0:1, 31:32], min_val=0, max_val=MAX_EXTRA)
                with act.Fori(0, MAX_EXTRA) as ub:
                    with act.If(n_more > ub):
                        act.wait_ge(o["xT_made"], ub + 1)
                        for k in range(KT):
                            last = A(xgT[:, k, :], ps[:, k // 4, (k % 4) * P:(k % 4 + 1) * P], ACT.Identity,
                                     scale=scale_col[:, u, k:k + 1], bias=shift_col[:, u, k:k + 1])
                        last.then_inc(o["xT_ready"], 1)
                        act.wait_ge(o["gu_done"], ub + 1)
                        A(hsil, ps[:, 2, :], ACT.Silu).then_inc(o["sil"], 1)
                        act.wait_ge(o["hT_made"], ub + 1)
                        A(hmidT, ps[:, 4, :].rearrange("p (a b) -> p a b", a=FT), ACT.Copy).then_inc(o["hmidT"], 1)
                        act.wait_ge(o["dn_done"], ub + 2)
                        A(yo[:, 0, 0:HALF], ps[:, 5, :], ACT.Copy).then_inc(o["yo_a"], 1)
                for i in range(TT):
                    n = TT * l + i
                    act.wait_ge(S[f"y_in{i % 2}"], 16 * (2 * l + i // 2 + 1))
                    if i == 0:
                        act.wait_ge(S["slots_ready"], l + 1)
                    else:
                        act.wait_ge(S["resid_ready"], 8 * l + 4 + max(i - 1, 0))
                    A(y_tmp[:, i % 2, :], y_pair[:, i % 2, 0:D], ACT.Copy, scale=wts[:, i, 0:1]
                      ).then_inc(S["y_first"], 1)
                if l == 0:
                    for n, g in mine("ada1", 5, "A"):
                        if n == 3:
                            act.wait_ge(S["resid_ready"], 8)
                        act.wait_ge(S["unit"], g + 1)
                        A(gate_bc[:, (n - 1) // 2, (n - 1) % 2 * HALF:((n - 1) % 2 + 1) * HALF], bank(g), ACT.Copy
                          ).then_inc(S["a_free"], 1)

        @block.vector
        def _(dve):
            then = in_order(dve, "dve_order")
            v = nc.vector

            def ada_half(n):
                ch, hf = divmod(n, 2)
                acc = gate_bc[:, ch % 2, :]
                dve.wait_ge(S[f"ada_in{n % 2}"], 16 * (n // 2 + 1))
                if counts(n):
                    dve.wait_ge(S["ada_used"], n)
                for k in range(4):
                    w = view(ring_gu0, (n % 2) * 4096 + k * D, D)
                    ck = c_act[:, 4 * hf + k:4 * hf + k + 1]
                    if hf == 0 and k == 0:
                        ins = v.tensor_scalar(acc, w, ck, None, ALU.mult)
                    else:
                        ins = v.scalar_tensor_tensor(out=acc, in0=w, scalar=ck, in1=acc, op0=ALU.mult, op1=ALU.add)
                    if k < 3:
                        then(ins)
                ins.then_inc(S["ada_used"], 1)

            def shift_out(u, g, col0, bias):
                dve.wait_ge(S["unit"], g + 1)
                src = bank(g)[:, col0:col0 + KT]
                if bias is None:
                    return v.tensor_copy(shift_col[:, u, :], src)
                return v.tensor_tensor(shift_col[:, u, :], src, bias, ALU.add)

            def scale_out(u, g, col0, bias):
                dve.wait_ge(S["unit"], g + 1)
                src = bank(g)[:, col0:col0 + KT]
                name = "norm_mix" if u % 2 == 0 else "norm_ffn"
                gain = vcols[:, VROW[name] + (u // 2) * KT:VROW[name] + (u // 2 + 1) * KT]
                if bias is not None:
                    then(v.tensor_tensor(scale_col[:, u, :], src, bias, ALU.add))
                    src = scale_col[:, u, :]
                return v.scalar_tensor_tensor(out=scale_col[:, u, :], in0=src, scalar=1.0, in1=gain,
                                              op0=ALU.add, op1=ALU.mult)

            def modulation0(u, stage, ch):
                g = STAGES[stage]
                b = [bcols[:, c2 * KT:(c2 + 1) * KT] for c2 in CHUNKS[ch:ch + 2]]
                shift_out(u, g, 0, b[0]).then_inc(S["d_free"], 1)
                scale_out(u, g + 1, 0, b[1]).then_inc(S["d_free"], 1)
                dve.wait_ge(S["d_free"], evacuated(g + 1)[1])
                dve.sem_inc(S["mod_ready"], 1)

            dve.wait_ge(S["c_ready"], 1)
            ada_half(0)
            ada_half(1)
            for n, (dst, width) in enumerate(((vcols, NVROW), (bcols, 48), (mcols, 7))):
                g = STAGES["setup"] + n
                dve.wait_ge(S["unit"], g + 1)
                v.tensor_copy(dst[:, :], bank(g)[:, 0:width]).then_inc(S["d_free"], 1)
            dve.wait_ge(S["d_free"], 3)
            for dr, name in enumerate(("lam_f", "lam_b")):
                lam = vcols[:, VROW[name]:VROW[name] + KT]
                part = slice(dr * KT, (dr + 1) * KT)
                then(v.tensor_scalar(lam_t[:, 2, part], lam, -1.0, 0.0, ALU.mult, ALU.max))
                then(v.tensor_scalar(lam_t[:, 3, part], lam, 0.0, None, ALU.max))
                then(v.tensor_tensor(lam_t[:, 0, part], lam_t[:, 2, part], lam_t[:, 3, part], ALU.add))
            v.tensor_copy(q_gain[0:QK, :], mcols[0:QK, 5:6]).then_inc(S["lam_abs"], 1)
            dve.wait_ge(S["lam_abs"], 1)
            v.tensor_scalar(q_gain[0:QK, :], q_gain[0:QK, :], float(QK) ** -0.5, None, ALU.mult
                            ).then_inc(S["cols_set"], 1)

            ada_half(2)
            ada_half(3)
            modulation0(0, "cols0", 0)

            def normalise(u):
                xn = NORM_XN[u]
                dve.wait_ge(S["ss_ready"], u + 1)
                then(v.reciprocal(rstd[:, :], std[:, :]))
                for i in range(TT):
                    v.tensor_scalar(xn[:, i, :], x_tok[:, i, :], rstd[:, i:i + 1], None, ALU.mult
                                    ).then_inc(S["xn_ready"], 1)

            def modulated(u):
                for k, g in mine(f"norm{u}", KT, "D"):
                    dve.wait_ge(S["unit"], g + 1)
                    v.tensor_scalar(hT[:, k, :], bank(g), scale_col[:, u, k:k + 1], shift_col[:, u, k:k + 1],
                                    ALU.mult, ALU.add).then_inc(S["d_free"], 1)

            normalise(0)
            modulated(0)
            for n, g in mine("lat", 8, "D"):
                dve.wait_ge(S["unit"], g + 1)
                v.tensor_copy(lat[:, n // 2, HALF:LAT], bank(g)[:, 0:LAT - HALF]).then_inc(S["d_free"], 1)
            dve.wait_ge(S["misc_in"], 16 * 4)
            dve.wait_ge(S["pool_const"], 1)
            then(v.tensor_copy(pos_f, pos_i[:, :]))
            then(v.tensor_tensor(trig[:, 0, :, :], pos_f.rearrange("p (i o) -> p i o", o=1).to_broadcast([P, TT, RH]),
                                 inv_freq.rearrange("p (o j) -> p o j", o=1).to_broadcast([P, TT, RH]), ALU.mult))
            for n, quarter in ((3, 0.0), (4, 0.25)):
                turns, rem = trig[:, 1, :, :], trig[:, n, :, :]
                then(v.tensor_scalar(turns, trig[:, 0, :, :], 1.0 / TWO_PI, quarter, ALU.mult, ALU.add))
                then(v.tensor_scalar(turns, turns, ROUNDER, None, ALU.add))
                then(v.tensor_scalar(turns, turns, ROUNDER, None, ALU.subtract))
                then(v.scalar_tensor_tensor(out=rem, in0=turns, scalar=-PI_PARTS[0], in1=trig[:, 0, :, :],
                                            op0=ALU.mult, op1=ALU.add))
                then(v.scalar_tensor_tensor(out=rem, in0=turns, scalar=-PI_PARTS[1], in1=rem,
                                            op0=ALU.mult, op1=ALU.add))
                then(v.scalar_tensor_tensor(out=rem, in0=turns, scalar=-PI_PARTS[2], in1=rem,
                                            op0=ALU.mult, op1=ALU.add))
                then(v.tensor_scalar(rem, rem, quarter * TWO_PI, PI_IN, ALU.add, ALU.min))
                if quarter:
                    v.tensor_scalar(rem, rem, -PI_IN, None, ALU.max).then_inc(S["angle_ready"], 1)
                else:
                    then(v.tensor_scalar(rem, rem, -PI_IN, None, ALU.max))
            dve.wait_ge(S["lat_stat"], 1)
            then(v.reciprocal(lat_r, lat_r))
            for i in range(TT):
                v.tensor_copy(k_pe_raw[:, i, :], lat[:, i, QL + KVL:LAT])
                v.tensor_scalar(lat[:, i, 0:QL], lat[:, i, 0:QL], lat_r[:, 0, i:i + 1], None, ALU.mult)
                last = v.tensor_scalar(lat[:, i, QL:QL + KVL], lat[:, i, QL:QL + KVL], lat_r[:, 1, i:i + 1], None,
                                       ALU.mult)
            last.then_inc(S["lat_scaled"], 1)
            for ch, g in mine("latT", 5, "D"):
                dve.wait_ge(S["unit"], g + 1)
                v.tensor_scalar(latT[:, ch, :], bank(g), mcols[:, ch:ch + 1], None, ALU.mult
                                ).then_inc(S["d_free"], 1)

            def rope_pairs(out1, out2, x1, x2, tabs, shape, t):
                c1, s2, s1, c2 = tabs
                then(v.tensor_tensor(t[0], x1, c1, ALU.mult))
                then(v.tensor_tensor(t[1], x2, s2, ALU.mult))
                then(v.tensor_tensor(t[2], x1, s1, ALU.mult))
                then(v.tensor_tensor(t[3], x2, c2, ALU.mult))
                then(v.tensor_tensor(out1, t[0], t[1], ALU.subtract))
                then(v.tensor_tensor(out2, t[2], t[3], ALU.add))

            dve.wait_ge(S["trig_ready"], 1)
            sin, cos = trig[:, 3, :, :], trig[:, 4, :, :]
            for n, tabs in enumerate(((rope_c1q, rope_s2q, rope_s1q, rope_c2q), (rope_c1k, rope_s2k, rope_s1k, rope_c2k))):
                for tab, fn, part in zip(tabs, (cos, sin, sin, cos), (0, 1, 0, 1)):
                    gain = ropeg[:, n:n + 1, part * RH:(part + 1) * RH].to_broadcast([P, TT, RH])
                    then(v.tensor_tensor(tab, fn, gain, ALU.mult))
            for i in range(TT):
                ada_half(4 + i)
                dve.wait_ge(S["sq_ready"], i + 1)
                v.tensor_reduce(rq[:, i, :], sq_tmp[:, i % 2, :].rearrange("p (h d) -> p h d", h=H), AX.X, ALU.add
                                ).then_inc(S["sq_used"], 1)
            modulation0(1, "ffncols0", 2)
            qx1, qx2 = q_tok[:, :, :, NOPE:NOPE + RH], q_tok[:, :, :, NOPE + RH:QK]
            wide = [t.rearrange("p i (o j) -> p i o j", o=1).to_broadcast([P, TT, H, RH])
                    for t in (rope_c1q, rope_s2q, rope_s1q, rope_c2q)]
            qt_ = [rope_tmp[:, n, :].rearrange("p (i h j) -> p i h j", i=TT, h=H) for n in range(4)]
            rope_pairs(qx1, qx2, qx1, qx2, wide, None, qt_)
            dve.sem_inc(S["ropeq_done"], 1)
            ada_half(8)
            ada_half(9)
            kt_ = [rope_k_tmp[:, n, :].rearrange("p (i j) -> p i j", i=TT) for n in range(4)]
            then(v.tensor_tensor(k_pe, k_pe_raw, k_pe_raw, ALU.mult))
            then(v.tensor_reduce(pe_ss, k_pe, AX.X, ALU.add))
            rope_pairs(k_pe[:, :, 0:RH], k_pe[:, :, RH:ROPE], k_pe_raw[:, :, 0:RH], k_pe_raw[:, :, RH:ROPE],
                       (rope_c1k, rope_s2k, rope_s1k, rope_c2k), None, kt_)
            for i in range(TT):
                dve.wait_ge(S["sq_ready"], TT + i + 1)
                v.tensor_reduce(rk[:, i, :], sq_tmp[:, i % 2, 0:H * NOPE].rearrange("p (h d) -> p h d", h=H),
                                AX.X, ALU.add).then_inc(S["sq_used"], 1)
                dve.wait_ge(S["sq_used"], TT + i + 1)
                ins = v.tensor_scalar(rk[:, i, :], rk[:, i, :], pe_ss[:, i:i + 1], None, ALU.add)
                if i < TT - 1:
                    then(ins)
                if i < 2:
                    ada_half(10 + i)
            ins.then_inc(S["qk_var"], 1)
            dve.wait_ge(S["qk_std"], 1)
            v.reciprocal(rq, rq)
            v.reciprocal(rk, rk).then_inc(S["rope_done"], 1)
            for n, g in mine("gate0", 4, "D"):
                dve.wait_ge(S["unit"], g + 1)
                v.tensor_copy(gate_bc[:, n // 2, n % 2 * HALF:(n % 2 + 1) * HALF], bank(g)).then_inc(S["d_free"], 1)

            def k_out(h, hb):
                dve.wait_ge(S["qkT_made"], h + 1)
                v.tensor_scalar(kT[0:QK, hb, :], ps[0:QK, 1, :], mcols[0:QK, 6:7], None, ALU.mult
                                ).then_inc(S["kT_ready"], 1)

            def head_step(it, p, last_pair=False, tail=False):
                s = it * 8 + p
                if not tail:
                    dve.wait_ge(S["s_ready"], s + 1)
                    v.tensor_reduce(nmax[:, p % 4:p % 4 + 1], ps[:, 2 + p % 4, :], AX.X, ALU.max, negate=True
                                    ).then_inc(S["nmax_ready"], 1)
                if p % 2 == 1 and not (isinstance(s, int) and (s < 2 or s >= NSTEP + 2)):
                    dve.wait_ge(S["pT_made"], s - 1)
                    if counts(s - 3):
                        dve.wait_ge(S["pv_done"], s - 3)
                    v.tensor_copy(probsT[:, 1, :, :], ps[:, 6, :].rearrange("p (a b) -> p a b", a=TT)
                                  ).then_inc(S["pT_d"], 1)
                if p % 4 == 2 and not tail and not (last_pair and p == 6):
                    k_out(it * 2 + p // 4 + 1, (p // 4 + 1) % 2)
                if p % 4 == 2 and not (isinstance(s, int) and s < 6):
                    hv = it * 2 + p // 4 - 1
                    dve.wait_ge(S["p_ready"], s - 2)
                    v.reciprocal(rrec, rsum[:, (p // 4 + 1) % 2, :]).then_inc(S["rrec_ready"], 1)
                    dve.wait_ge(S["rrec_ready"], hv + 1)
                    dve.wait_ge(S["pv_done"], s - 2)
                    v.tensor_tensor(o_heads[:, :, at(hv), :].rearrange("p i o d -> p i (o d)"),
                                    ps[:, 7, 0:TT * VH].rearrange("p (i d) -> p i d", i=TT),
                                    rrec.rearrange("p (i o) -> p i o", o=1).to_broadcast([P, TT, VH]), ALU.mult
                                    ).then_inc(S["o_done"], 1)

            k_out(0, 0)
            for p in range(8):
                head_step(0, p)
            with dve.Fori(1, H // 2 - 1) as it:
                for p in range(8):
                    head_step(it, p)
            for p in range(8):
                head_step(H // 2 - 1, p, last_pair=True)
            for p in range(3):
                head_step(H // 2, p, tail=True)
            for k, g in mine("oT", 8, "D"):
                dve.wait_ge(S["unit"], g + 1)
                v.tensor_copy(oT[:, k, :], bank(g)).then_inc(S["d_free"], 1)
            dve.wait_ge(S["lam_exp"], 1)
            e_, z, z2, ser = lam_t[:, 1, :], lam_t[:, 0, :], lam_t[:, 3, :], lam_c.rearrange("p a b -> p (a b)")
            then(v.tensor_scalar(z, e_, 2.0, None, ALU.add))
            then(v.reciprocal(z, z))
            then(v.tensor_tensor(z, z, e_, ALU.mult))
            then(v.tensor_tensor(z2, z, z, ALU.mult))
            then(v.tensor_scalar(ser, z2, 1.0 / 17, 1.0 / 15, ALU.mult, ALU.add))
            for odd in (13, 11, 9, 7, 5, 3, 1):
                then(v.tensor_tensor(ser, ser, z2, ALU.mult))
                then(v.tensor_scalar(ser, ser, 1.0 / odd, None, ALU.add))
            then(v.tensor_tensor(ser, ser, z, ALU.mult))
            then(v.scalar_tensor_tensor(out=ser, in0=ser, scalar=2.0, in1=lam_t[:, 2, :], op0=ALU.mult, op1=ALU.add))
            then(v.tensor_scalar(ser, ser, LRU_C / 2, None, ALU.mult))

            def residual(l):
                for i in range(TT):
                    for hf in range(2):
                        g = STAGES[f"proj{l}"] + 2 * i + hf
                        part = slice(hf * HALF, (hf + 1) * HALF)
                        dve.wait_ge(S["unit"], g + 1)
                        v.tensor_tensor(prod[:, hf, :], bank(g), gate_bc[:, 0, part], ALU.mult
                                        ).then_inc(S["d_free"], 1)
                        dve.wait_ge(S["d_free"], evacuated(g)[1])
                        ins = v.tensor_tensor(x_tok[:, i, part], x_tok[:, i, part], prod[:, hf, :], ALU.add)
                    ins.then_inc(S["resid_ready"], 1)

            for l in range(2):
                if l == 1:
                    normalise(2)
                    modulated(2)
                    dve.wait_ge(S["unit"], STAGES["norm2"] + 8)
                    then(v.memset(xb_pad[:, :, 0:2], 0.0))
                    then(v.memset(xb_pad[:, :, pad - 1:pad], 0.0))

                    def convolution(b):
                        xc = xc_[b % 2]
                        if counts(b - 1):
                            dve.wait_ge(S["unit"], STAGES[f"rg{b - 2}"] + 8)
                        if counts(b):
                            dve.wait_ge(S["xc_ready"], b)
                        for m, g in mine(f"xb{b}", 2, "D"):
                            dve.wait_ge(S["unit"], g + 1)
                            v.tensor_copy(xb_pad[:, m, 2:2 + SEQ], bank(g)).then_inc(S["d_free"], 1)
                        dve.wait_ge(S["d_free"], evacuated(STAGES[f"xb{b}"] + 1)[1])
                        for tap in range(4):
                            for m in range(2):
                                ch = 2 * b + m
                                w = vcols[:, VROW["conv_w"] + tap * KT + ch:VROW["conv_w"] + tap * KT + ch + 1]
                                src = xb_pad[:, m, tap:tap + SEQ]
                                if tap == 0:
                                    bias = vcols[:, VROW["conv_b"] + ch:VROW["conv_b"] + ch + 1]
                                    ins = v.tensor_scalar(xc[:, m, :], src, w, bias, ALU.mult, ALU.add)
                                else:
                                    ins = v.scalar_tensor_tensor(out=xc[:, m, :], in0=src, scalar=w, in1=xc[:, m, :],
                                                                 op0=ALU.mult, op1=ALU.add)
                                if tap < 3:
                                    then(ins)
                        ins.then_inc(S["xc_ready"], 1)

                    convolution(0)
                    for b in range(NBLK):
                        if b < NBLK - 1:
                            convolution(b + 1)
                        xc, gate_s = xc_[b % 2], gate_[b % 2]
                        dve.wait_ge(S["t_ready"], b + 1)
                        v.tensor_scalar(rc_s, t_s, 1.0, None, ALU.add).then_inc(S["rc_ready"], 1)
                        dve.wait_ge(S["rc_ready"], b + 1)
                        then(v.reciprocal(rc_s, rc_s))
                        then(v.tensor_scalar(r_s, rc_s, 2.0, -1.0, ALU.mult, ALU.add))
                        for dr in range(2):
                            part = slice(2 * dr, 2 * dr + 2)
                            first = slice(SEQ - 1, SEQ) if dr else slice(0, 1)
                            then(v.tensor_tensor(i_s[:, part, :], i_s[:, part, :], xc, ALU.mult))
                            then(v.tensor_copy(first_s[:, part], i_s[:, part, first].rearrange("p m o -> p (m o)")))
                            then(v.scalar_tensor_tensor(out=i_s[:, part, :], in0=i_s[:, part, :], scalar=2.0,
                                                        in1=rc_s[:, part, :], op0=ALU.mult, op1=ALU.mult))
                            dve.wait_ge(S["st_ready"], b + 1)
                            then(v.tensor_tensor(i_s[:, part, :], i_s[:, part, :], t_s[:, part, :], ALU.mult))
                            then(v.tensor_copy(i_s[:, part, first].rearrange("p m o -> p (m o)"), first_s[:, part]))
                            for m in range(2):
                                n = 2 * dr + m
                                rev = slice(None, None, -1) if dr else slice(None)
                                then(v.tensor_tensor_scan(rc_s[:, n, rev], r_s[:, n, rev], i_s[:, n, rev], 0.0,
                                                          ALU.mult, ALU.add))
                        then(v.tensor_tensor(rc_s[:, 0:2, :], rc_s[:, 0:2, :], rc_s[:, 2:4, :], ALU.add))
                        dve.wait_ge(S["gelu_ready"], b + 1)
                        v.tensor_tensor(yT[:, 2 * b:2 * b + 2, :], rc_s[:, 0:2, :], gate_s, ALU.mult
                                        ).then_inc(S["y_ready"], 1)
                residual(l)
                normalise(2 * l + 1)
                modulated(2 * l + 1)

                flat = lambda t: t.rearrange("p i e -> p (i e)")
                dve.wait_ge(S["a_free"], evacuated(STAGES[f"logits{l}"])[1])
                dve.wait_ge(S["misc_in"], 64)
                then(v.tensor_tensor(biased[:, :, :], scores[:, :, :],
                                     rbias.rearrange("p (o e) -> p o e", o=1).to_broadcast([P, TT, NE]), ALU.add))
                quad = flat(biased).rearrange("p (g e) -> p g e", e=EPG)
                then(v.tensor_tensor(pairs[:, :, 0:3], quad[:, :, 0:3], quad[:, :, 1:4], ALU.add))
                then(v.tensor_tensor(pairs[:, :, 3:5], quad[:, :, 0:2], quad[:, :, 2:4], ALU.add))
                then(v.tensor_tensor(pairs[:, :, 5:6], quad[:, :, 0:1], quad[:, :, 3:4], ALU.add))
                then(v.tensor_reduce(flat(gs[:, 0, :, :]), pairs[:, :, :], AX.X, ALU.max))

                def along(t, n):
                    return t.rearrange("p (i o) -> p i o", o=1).to_broadcast([P, TT, n])

                def first_max(values, down, out, tmp, n, m1, m2):
                    then(v.tensor_reduce(m1, values, AX.X, ALU.max))
                    then(v.tensor_tensor(tmp, values, along(m1, n), ALU.is_equal))
                    then(v.tensor_tensor(tmp, tmp, down, ALU.mult))
                    then(v.tensor_reduce(m2, tmp, AX.X, ALU.max))
                    then(v.tensor_tensor(out, down, along(m2, n), ALU.is_equal))

                col = lambda n: rs_small[:, n, :]
                masked, off, one1, one2, tmp, rank_id, tmp2 = (rt[:, n, :, :] for n in range(7))
                first_max(gs[:, 0, :, :], down_g[:, :, :], gs[:, 2, :, :], gs[:, 1, :, :], NG, col(0), col(1))
                in_group = flat(gs[:, 2, :, :]).rearrange("p (g o) -> p g o", o=1).to_broadcast([P, TT * NG, EPG])
                as_quad = lambda t: flat(t).rearrange("p (g e) -> p g e", e=EPG)
                then(v.tensor_scalar(gs[:, 1, :, :], gs[:, 2, :, :], 1.0, FAR, ALU.subtract, ALU.mult))
                out_group = flat(gs[:, 1, :, :]).rearrange("p (g o) -> p g o", o=1).to_broadcast([P, TT * NG, EPG])
                then(v.tensor_tensor(as_quad(masked), quad, in_group, ALU.mult))
                then(v.tensor_tensor(as_quad(masked), as_quad(masked), out_group, ALU.add))
                first_max(masked, down_e[:, :, :], one1, tmp, NE, col(2), col(3))
                then(v.scalar_tensor_tensor(out=flat(masked), in0=flat(one1), scalar=-2.0 * FAR, in1=flat(masked),
                                            op0=ALU.mult, op1=ALU.add))
                first_max(masked, down_e[:, :, :], one2, tmp, NE, col(4), col(5))
                v.tensor_tensor(chosen[:, :, :], one1, one2, ALU.add).then_inc(S["chosen_ready"], 1)
                for k, one in enumerate((one1, one2)):
                    then(v.tensor_tensor(tmp, one, scores[:, :, :], ALU.mult))
                    then(v.tensor_reduce(col(6 + k), tmp, AX.X, ALU.add))
                then(v.tensor_tensor(col(8), col(6), col(7), ALU.add))
                then(v.reciprocal(col(8), col(8)))
                for k in range(2):
                    then(v.tensor_tensor(wts[:, :, k], col(6 + k), col(8), ALU.mult))
                g = STAGES[f"rank{l}"]
                dve.wait_ge(S["unit"], g + 1)
                v.scalar_tensor_tensor(out=flat(rank_id), in0=bank(g)[:, 0:TT * NE], scalar=float(NE),
                                       in1=flat(up_e), op0=ALU.mult, op1=ALU.add).then_inc(S["d_free"], 1)
                dve.wait_ge(S["d_free"], evacuated(g)[1])
                for k, one in enumerate((one1, one2)):
                    then(v.tensor_tensor(tmp, one, rank_id, ALU.mult))
                    then(v.tensor_reduce(col(9 + k), tmp, AX.X, ALU.add))
                v.tensor_copy(dest[:, :, 0], col(9))
                v.tensor_copy(dest[:, :, 1], col(10)).then_inc(S["dest_ready"], 1)
                dve.wait_ge(S["unit"], g + 2)
                ins = v.tensor_copy(more[:, 0, 0:NE], bank(g + 1)[0:1, 0:NE])
                ins.then_inc(S["d_free"], 1)
                dve.wait_ge(S["d_free"], evacuated(g + 1)[1])
                flag, cum, fid, hit = (more[:, n, :] for n in (1, 2, 3, 4))
                for j in range(3):
                    then(v.tensor_scalar(flag[:, j * NE:(j + 1) * NE], more[:, 0, 0:NE], float(P * (j + 1)), None,
                                         ALU.is_gt))
                then(v.memset(more[:, 5, :], 1.0))
                then(v.tensor_tensor_scan(cum, more[:, 5, :], flag, 0.0, ALU.mult, ALU.add))
                then(v.tensor_tensor(fid, flag, more_id[0:1, :], ALU.mult))
                then(v.memset(more_f[:, :], 0.0))
                for n in range(MAX_EXTRA):
                    then(v.scalar_tensor_tensor(out=hit, in0=cum, scalar=float(n + 1), in1=fid,
                                                op0=ALU.is_equal, op1=ALU.mult))
                    then(v.tensor_reduce(more_f[:, n:n + 1], hit, AX.X, ALU.max))
                then(v.tensor_copy(more_f[:, 31:32], cum[:, 3 * NE - 1:3 * NE]))
                then(v.tensor_copy(more_i[:, :], more_f[:, :]))
                then(v.tensor_scalar(more_i[:, 16:16 + MAX_EXTRA], more_i[:, 0:MAX_EXTRA], NE - 1, None,
                                     ALU.bitwise_and))
                dve.wait_ge(S["table_in"], 16 * (l + 1))
                v.tensor_scalar(slot_tok[:, :, :], slot_val[:, :, :], 1, None, ALU.logical_shift_right
                                ).then_inc(S["slots_ready"], 1)

                base = NE * l
                u = 2 * l + 1

                def rows_out(e):
                    dve.wait_ge(S["xT_made"], e + 1)
                    for k in range(4, KT):
                        last = v.tensor_scalar(xgT[:, k, :], ps[:, 1, (k - 4) * P:(k - 3) * P],
                                               scale_col[:, u, k:k + 1], shift_col[:, u, k:k + 1],
                                               ALU.mult, ALU.add)
                    last.then_inc(S["xT_d"], 1)

                def down_out(pair_no, q, e):
                    if counts((pair_no + NPAIR * l) * 16):
                        dve.wait_ge(S[f"scattered{q}"], (pair_no + NPAIR * l) * 16)
                    dve.wait_ge(S["dn_done"], e + 1)
                    v.tensor_copy(yo[:, q, HALF:D], ps[:, 6, :]).then_inc(S["yo_d"], 1)

                def expert(it, q, first=False, last=False):
                    e = it * 2 + q + base
                    dve.wait_ge(S["sil_ready"], e + 1)
                    if counts(e):
                        dve.wait_ge(S["hT_made"], e)
                    v.tensor_tensor(hmid, hsil, ps[:, 3, :], ALU.mult).then_inc(S["hmid_ready"], 1)
                    if not last:
                        rows_out(e + 1)
                    if not first:
                        down_out(it if q else it - 1, 1 - q, e - 1)

                def ada_row(k, o):
                    dve.wait_ge(S[f"stage_in{o}"], k * 16 + 16)
                    if counts(k * 2 + o - 1):
                        dve.wait_ge(S["stage_used"], k * 2 + o - 1)
                    v.scalar_tensor_tensor(out=acc1[:, o, :], in0=stage[:, o, :], scalar=c_act[:, at(k)],
                                           in1=acc1[:, o, :], op0=ALU.mult, op1=ALU.add
                                           ).then_inc(S["stage_used"], 1)

                rows_out(base)
                if l == 0:
                    dve.wait_ge(S["acc1_bias"], 16)
                expert(0, 0, first=True)
                expert(0, 1)
                if l == 0:
                    ada_row(0, 0)
                expert(1, 0)
                expert(1, 1)
                if l == 0:
                    ada_row(0, 1)
                with dve.Fori(1, NPAIR // 2 - 1) as it2:
                    for o in range(2):
                        expert(it2 * 2 + o, 0)
                        expert(it2 * 2 + o, 1)
                        if l == 0:
                            ada_row(it2, o)
                expert(NPAIR - 2, 0)
                expert(NPAIR - 2, 1)
                if l == 0:
                    ada_row(KT - 1, 0)
                expert(NPAIR - 1, 0)
                expert(NPAIR - 1, 1, last=True)
                if l == 0:
                    ada_row(KT - 1, 1)
                down_out(NPAIR - 1, 1, base + NE - 1)
                o = OV[l]
                dve.wait_ge(S["slots_ready"], l + 1)
                dve.wait_ge(S["scattered0"], 16 * NPAIR * (l + 1))
                n_more = dve.value_load(more_i[0:1, 31:32], min_val=0, max_val=MAX_EXTRA)
                with dve.Fori(0, MAX_EXTRA) as ub:
                    with dve.If(n_more > ub):
                        dve.wait_ge(o["sil"], ub + 1)
                        v.tensor_tensor(hmid, hsil, ps[:, 3, :], ALU.mult).then_inc(o["hmid"], 1)
                        dve.wait_ge(o["dn_done"], ub + 2)
                        v.tensor_copy(yo[:, 0, HALF:D], ps[:, 6, :]).then_inc(o["yo_d"], 1)
                if l == 0:
                    g = STAGES["ada1"]
                    then(shift_out(2, g, 0, None))
                    then(scale_out(2, g, KT, None))
                    then(shift_out(3, g, 2 * KT, None))
                    scale_out(3, g, 3 * KT, None).then_inc(S["d_free"], 1)
                    dve.wait_ge(S["d_free"], evacuated(g)[1])
                    dve.sem_inc(S["mod_ready"], 2)
                for i in range(TT):
                    n = TT * l + i
                    t = y_tmp[:, i % 2, :]
                    dve.wait_ge(S["y_first"], n + 1)
                    v.scalar_tensor_tensor(out=t, in0=y_pair[:, i % 2, D:2 * D], scalar=wts[:, i, 1:2], in1=t,
                                           op0=ALU.mult, op1=ALU.add).then_inc(S["y_used"], 1)
                    dve.wait_ge(S["y_used"], n + 1)
                    then(v.tensor_tensor(t, t, gate_bc[:, 1, :], ALU.mult))
                    v.tensor_tensor(x_tok[:, i, :], x_tok[:, i, :], t, ALU.add).then_inc(S["resid_ready"], 1)


_INS = ['x', 'c', 'positions', 'norm_mix', 'norm_ffn', 'w_ada', 'b_ada', 'mla_w_in', 'mla_q_a_norm', 'mla_kv_a_norm',
        'mla_w_q_b', 'mla_w_kv_b', 'mla_q_norm', 'mla_k_norm', 'mla_w_o', 'rnn_w_in', 'rnn_conv_w', 'rnn_conv_b',
        'rnn_lam_f', 'rnn_w_rf', 'rnn_b_rf', 'rnn_w_if', 'rnn_b_if', 'rnn_lam_b', 'rnn_w_rb', 'rnn_b_rb', 'rnn_w_ib',
        'rnn_b_ib', 'rnn_w_o', 'w_router', 'router_bias', 'moe_w_gu', 'moe_w_dn']
_OUTS = [((1, 512, 1024), 'float32')]


def kernel(**inputs):
    import numpy as _np
    import concourse.bacc as _bacc
    from concourse import mybir as _mybir
    from concourse.bass_utils import run_bass_kernel_spmd as _run

    nc = _bacc.Bacc("TRN2", target_bir_lowering=False, num_devices=1)
    arrays, args = {}, []
    for name in _INS:
        a = _np.ascontiguousarray(inputs[name])
        arrays[f"in_{name}_dram"] = a
        args.append(nc.dram_tensor(f"in_{name}_dram", a.shape, _mybir.dt.from_np(a.dtype), kind="ExternalInput").ap())
    for i, (shape, dtype) in enumerate(_OUTS):
        dt = _mybir.dt.from_np(_np.dtype(dtype))
        args.append(nc.dram_tensor(f"out_{i}_dram", shape, dt, kind="ExternalOutput").ap())
    trunk(nc, *args)
    r = _run(nc, [arrays], core_ids=[0])
    got = tuple(r.results[0][f"out_{i}_dram"] for i in range(len(_OUTS)))
    return got[0]
```
